# Optimizing a Trainium2 kernel written in Bass

```python
import math
import jax, jax.numpy as jnp
from jax import lax
import numpy as np

D_MODEL = 1024
BATCH = 1
SEQ = 512
DEPTH = 1

CHUNK = 64
EPS = 1e-6

SSD_WIDTH = D_MODEL // 2
SSD_HEAD_DIM = 64
SSD_HEADS = SSD_WIDTH // SSD_HEAD_DIM
SSD_GROUPS = 2
SSD_HEADS_PER_GROUP = SSD_HEADS // SSD_GROUPS
SSD_STATE = 128
CONV_WIDTH = 4
SSD_CONV_CH = SSD_WIDTH + 2 * SSD_GROUPS * SSD_STATE

DIFF_WIDTH = D_MODEL - SSD_WIDTH
DIFF_HEADS = 4
DIFF_VDIM = DIFF_WIDTH // DIFF_HEADS
DIFF_QKDIM = DIFF_VDIM // 2
ROPE_DIM = DIFF_QKDIM // 4
ROPE_THETA = 500000.0
Q_BLOCK = 128

QK_COLS = DIFF_HEADS * 2 * DIFF_QKDIM
SPLITS = (SSD_WIDTH,
          SSD_WIDTH + SSD_CONV_CH,
          SSD_WIDTH + SSD_CONV_CH + SSD_HEADS,
          SSD_WIDTH + SSD_CONV_CH + SSD_HEADS + QK_COLS,
          SSD_WIDTH + SSD_CONV_CH + SSD_HEADS + 2 * QK_COLS)
IN_COLS = SPLITS[-1] + DIFF_WIDTH
MIX_WIDTH = SSD_WIDTH + DIFF_WIDTH

PEER_HEADS = 8
N_KEYS = 128
N_EXPERTS = N_KEYS * N_KEYS
PEER_KEY_DIM = 256
PEER_HALF = PEER_KEY_DIM // 2
PEER_TOPK = 16
PEER_TOKEN_BLOCK = 128

kernel_name = "hybrid_ssd_diffattn_peer_block"

def rmsnorm(x, w):
    xf = x.astype(jnp.float32)
    y = xf * lax.rsqrt(jnp.mean(xf * xf, axis=-1, keepdims=True) + EPS)
    return (y * w.astype(jnp.float32)).astype(x.dtype)

def rotary_tables(seq):
    inv = jnp.power(ROPE_THETA, -jnp.arange(0, ROPE_DIM, 2, dtype=jnp.float32) / ROPE_DIM)
    ang = jnp.arange(seq, dtype=jnp.float32)[:, None] * inv[None, :]
    return jnp.cos(ang), jnp.sin(ang)

def partial_rotary(x, cos, sin):
    half = ROPE_DIM // 2
    c = cos[:, None, None, :]
    s = sin[:, None, None, :]
    xf = x.astype(jnp.float32)
    x1, x2, xp = xf[..., :half], xf[..., half:ROPE_DIM], xf[..., ROPE_DIM:]
    out = jnp.concatenate([x1 * c - x2 * s, x1 * s + x2 * c, xp], axis=-1)
    return out.astype(x.dtype)

def causal_depthwise_conv(u, w, b):
    out = lax.conv_general_dilated(
        u, w[:, None, :].astype(u.dtype), window_strides=(1,),
        padding=[(CONV_WIDTH - 1, 0)],
        dimension_numbers=('NWC', 'WIO', 'NWC'),
        feature_group_count=u.shape[-1])
    return out + b.astype(u.dtype)

def ssd_branch(z, xbc, dt_raw, conv_w, conv_b, dt_bias, a_log, d_skip, norm_w):
    f32 = jnp.float32
    b, s, _ = z.shape
    nc = s // CHUNK
    G, HG = SSD_GROUPS, SSD_HEADS_PER_GROUP
    xbc = jax.nn.silu(causal_depthwise_conv(xbc, conv_w, conv_b))
    xs, bm, cm = jnp.split(xbc, [SSD_WIDTH, SSD_WIDTH + G * SSD_STATE], axis=-1)
    xs = xs.reshape(b, nc, CHUNK, G, HG, SSD_HEAD_DIM).astype(f32)
    bm = bm.reshape(b, nc, CHUNK, G, SSD_STATE).astype(f32)
    cm = cm.reshape(b, nc, CHUNK, G, SSD_STATE).astype(f32)
    dt = jax.nn.softplus(dt_raw.astype(f32) + dt_bias.astype(f32)).reshape(b, nc, CHUNK, G, HG)
    a = -jnp.exp(a_log.astype(f32)).reshape(G, HG)
    a_cs = jnp.cumsum(dt * a, axis=2)
    xdt = xs * dt[..., None]
    seg = a_cs[:, :, :, None] - a_cs[:, :, None, :]
    causal = jnp.tril(jnp.ones((CHUNK, CHUNK), dtype=bool))[:, :, None, None]
    decay = jnp.exp(jnp.where(causal, seg, -jnp.inf))
    cb = jnp.einsum('bclgn,bcsgn->bclsg', cm, bm)
    y_diag = jnp.einsum('bclsg,bclsgh,bcsghp->bclghp', cb, decay, xdt)
    decay_to_end = jnp.exp(a_cs[:, :, -1:] - a_cs)
    states = jnp.einsum('bclgn,bclgh,bclghp->bcghpn', bm, decay_to_end, xdt)
    chunk_decay = jnp.exp(a_cs[:, :, -1])

    def step(carry, inp):
        st, dc = inp
        return carry * dc[..., None, None] + st, carry

    init = jnp.zeros_like(states[:, 0])
    _, prev = lax.scan(step, init, (jnp.moveaxis(states, 1, 0), jnp.moveaxis(chunk_decay, 1, 0)))
    prev = jnp.moveaxis(prev, 0, 1)
    y_off = jnp.einsum('bclgn,bcghpn,bclgh->bclghp', cm, prev, jnp.exp(a_cs))
    y = y_diag + y_off + xs * d_skip.astype(f32).reshape(G, HG)[:, :, None]
    y = y.reshape(b, s, SSD_WIDTH)
    y = (y * jax.nn.silu(z.astype(f32))).reshape(b, s, G, SSD_WIDTH // G)
    y = y * lax.rsqrt(jnp.mean(y * y, axis=-1, keepdims=True) + EPS)
    y = y.reshape(b, s, SSD_WIDTH) * norm_w.astype(f32)
    return y.astype(z.dtype)

def diff_attention(q, k, v, qn_w, kn_w, lq1, lk1, lq2, lk2, subln_w, lambda_init, cos, sin):
    f32 = jnp.float32
    b, s, _ = q.shape
    nb = s // Q_BLOCK
    q = q.reshape(b, s, DIFF_HEADS, 2, DIFF_QKDIM)
    k = k.reshape(b, s, DIFF_HEADS, 2, DIFF_QKDIM)
    vf = v.reshape(b, s, DIFF_HEADS, DIFF_VDIM).astype(f32)
    q = partial_rotary(rmsnorm(q, qn_w), cos, sin).astype(f32)
    kf = partial_rotary(rmsnorm(k, kn_w), cos, sin).astype(f32)
    lam = (jnp.exp(jnp.sum(lq1.astype(f32) * lk1.astype(f32)))
           - jnp.exp(jnp.sum(lq2.astype(f32) * lk2.astype(f32))) + lambda_init)
    qb = jnp.moveaxis(q.reshape(b, nb, Q_BLOCK, DIFF_HEADS, 2, DIFF_QKDIM), 1, 0)
    k_chunk = jnp.arange(s) // CHUNK
    scale = DIFF_QKDIM ** -0.5

    def block(args):
        qi, i = args
        q_chunk = (i * Q_BLOCK + jnp.arange(Q_BLOCK)) // CHUNK
        mask = k_chunk[None, :] <= q_chunk[:, None]
        sc = jnp.einsum('bqhjd,bkhjd->bhjqk', qi, kf) * scale
        p = jax.nn.softmax(jnp.where(mask, sc, -jnp.inf), axis=-1)
        attn = p[:, :, 0] - lam * p[:, :, 1]
        return jnp.einsum('bhqk,bkhd->bqhd', attn, vf)

    o = lax.map(block, (qb, jnp.arange(nb)))
    o = jnp.moveaxis(o, 0, 1).reshape(b, s, DIFF_HEADS, DIFF_VDIM)
    o = rmsnorm(o, subln_w) * (1.0 - lambda_init)
    return o.reshape(b, s, DIFF_WIDTH).astype(v.dtype)

def peer_ffn(x, w_q, sub_keys, u, v):
    f32 = jnp.float32
    b, s, d = x.shape
    tb = PEER_TOKEN_BLOCK
    xt = x.reshape((b * s) // tb, tb, d)
    K = PEER_TOPK

    def block(xb):
        q = (xb @ w_q).reshape(tb, PEER_HEADS, 2, PEER_HALF).astype(f32)
        sc = jnp.einsum('thjd,hjnd->thjn', q, sub_keys.astype(f32))
        s_half, i_half = lax.top_k(sc, K)
        cand = (s_half[:, :, 0, :, None] + s_half[:, :, 1, None, :]).reshape(tb, PEER_HEADS, K * K)
        cand_idx = (i_half[:, :, 0, :, None] * N_KEYS + i_half[:, :, 1, None, :]).reshape(tb, PEER_HEADS, K * K)
        top_s, top_pos = lax.top_k(cand, K)
        idx = jnp.take_along_axis(cand_idx, top_pos, axis=-1)
        g = jax.nn.softmax(top_s, axis=-1)
        u_sel = u[idx]
        v_sel = v[idx]
        h = jax.nn.gelu(jnp.einsum('td,thkd->thk', xb, u_sel).astype(f32), approximate=False)
        return jnp.einsum('thk,thkd->td', (g * h).astype(xb.dtype), v_sel)

    out = lax.map(block, xt)
    return out.reshape(b, s, d).astype(x.dtype)

def setup_inputs(seed: int = 0) -> dict:
    key = jax.random.key(seed)
    ks = jax.random.split(key, 24)
    f32 = jnp.float32
    nrm = lambda k, shape, sc: jax.random.normal(k, shape, f32) * sc
    L = DEPTH
    dt0 = jnp.exp(jax.random.uniform(ks[5], (L, SSD_HEADS), f32) * (math.log(0.1) - math.log(0.001)) + math.log(0.001))
    return {
        'x': nrm(ks[0], (BATCH, SEQ, D_MODEL), 1.0),
        'mix_norm_w': 1.0 + nrm(ks[1], (L, D_MODEL), 0.05),
        'w_in': nrm(ks[2], (L, D_MODEL, IN_COLS), D_MODEL ** -0.5),
        'conv_w': nrm(ks[3], (L, CONV_WIDTH, SSD_CONV_CH), CONV_WIDTH ** -0.5),
        'conv_b': nrm(ks[4], (L, SSD_CONV_CH), 0.02),
        'dt_bias': dt0 + jnp.log(-jnp.expm1(-dt0)),
        'a_log': jnp.log(jax.random.uniform(ks[6], (L, SSD_HEADS), f32, 1.0, 16.0)),
        'd_skip': 1.0 + nrm(ks[7], (L, SSD_HEADS), 0.1),
        'ssd_norm_w': 1.0 + nrm(ks[8], (L, SSD_WIDTH), 0.05),
        'q_norm_w': 1.0 + nrm(ks[9], (L, DIFF_QKDIM), 0.05),
        'k_norm_w': 1.0 + nrm(ks[10], (L, DIFF_QKDIM), 0.05),
        'lambda_q1': nrm(ks[11], (L, DIFF_QKDIM), 0.1),
        'lambda_k1': nrm(ks[12], (L, DIFF_QKDIM), 0.1),
        'lambda_q2': nrm(ks[13], (L, DIFF_QKDIM), 0.1),
        'lambda_k2': nrm(ks[14], (L, DIFF_QKDIM), 0.1),
        'subln_w': 1.0 + nrm(ks[15], (L, DIFF_VDIM), 0.05),
        'w_out': nrm(ks[16], (L, MIX_WIDTH, D_MODEL), MIX_WIDTH ** -0.5),
        'ffn_norm_w': 1.0 + nrm(ks[17], (L, D_MODEL), 0.05),
        'peer_w_q': nrm(ks[18], (L, D_MODEL, PEER_HEADS * PEER_KEY_DIM), D_MODEL ** -0.5),
        'peer_sub_keys': nrm(ks[19], (L, PEER_HEADS, 2, N_KEYS, PEER_HALF), PEER_HALF ** -0.5),
        'peer_u': nrm(ks[20], (L, N_EXPERTS, D_MODEL), D_MODEL ** -0.5),
        'peer_v': nrm(ks[21], (L, N_EXPERTS, D_MODEL), 0.5),
    }

def reference(x, mix_norm_w, w_in, conv_w, conv_b, dt_bias, a_log, d_skip, ssd_norm_w,
              q_norm_w, k_norm_w, lambda_q1, lambda_k1, lambda_q2, lambda_k2, subln_w,
              w_out, ffn_norm_w, peer_w_q, peer_sub_keys, peer_u, peer_v):
    cos, sin = rotary_tables(x.shape[1])
    for layer in range(DEPTH):
        lambda_init = 0.8 - 0.6 * math.exp(-0.3 * layer)
        hn = rmsnorm(x, mix_norm_w[layer])
        proj = hn @ w_in[layer]
        z, xbc, dt_raw, q, k, v = jnp.split(proj, SPLITS, axis=-1)
        y_ssd = ssd_branch(z, xbc, dt_raw, conv_w[layer], conv_b[layer], dt_bias[layer],
                           a_log[layer], d_skip[layer], ssd_norm_w[layer])
        y_diff = diff_attention(q, k, v, q_norm_w[layer], k_norm_w[layer], lambda_q1[layer],
                                lambda_k1[layer], lambda_q2[layer], lambda_k2[layer],
                                subln_w[layer], lambda_init, cos, sin)
        x = x + jnp.concatenate([y_ssd, y_diff], axis=-1) @ w_out[layer]
        x = x + peer_ffn(rmsnorm(x, ffn_norm_w[layer]), peer_w_q[layer], peer_sub_keys[layer],
                         peer_u[layer], peer_v[layer])
    return x


_drawn_inputs = setup_inputs


def setup_inputs(seed=0):
    import zlib

    import numpy as np

    out = dict(_drawn_inputs(seed))
    spreads = {}
    factors = {}
    for name, (base, spread) in spreads.items():
        noise = np.random.default_rng([zlib.crc32(name.encode()), seed]).standard_normal(out[name].shape)
        drawn = base * np.exp(spread * noise) if base else spread * noise
        out[name] = __import__('jax').numpy.asarray(drawn.astype(out[name].dtype))
    for name, factor in factors.items():
        out[name] = (out[name] * factor).astype(out[name].dtype)
    return out
```

```python
import math
import numpy as np
import concourse.bass as bass
from concourse import mybir
from contextlib import ExitStack

F32 = mybir.dt.float32
I32 = mybir.dt.int32
U32 = mybir.dt.uint32
ALU = mybir.AluOpType
ACT = mybir.ActivationFunctionType
AXX = mybir.AxisListType.X

P = 128
SEQ, DM = 512, 1024
NB = SEQ // P
KC = DM // P
HALF = 512
SSDW, HD, NH, NG, NST = 512, 64, 8, 2, 128
HPG = NH // NG
CONVW, CONVC = 4, 1024
CB = CONVC // P
DH, QKD, VD = 4, 64, 128
RD = 8
EPS = 1e-6
LAMBDA_INIT = 0.8 - 0.6 * math.exp(-0.3 * 0)
PH, TOPK, NKEY, NEXP = 8, 16, 128, 128 * 128
NSLOT = PH * TOPK
NEG = -3.0e38
NHALFW = 4
RING = 8
COL_Z, COL_XBC, COL_DT, COL_Q, COL_K, COL_V = 0, 512, 1536, 1544, 2056, 2568

R_DTB, R_ALOG, R_D, R_QN, R_KN, R_L = 0, 8, 16, 24, 88, 152
NROW = R_L + 4 * 64
C_ID, C_TRI, C_COS, C_SIN, C_IOTA = 0, 128, 256, 256 + NB * RD, 256 + 2 * NB * RD
NCONST = C_IOTA + 16
V_MIX, V_SSD, V_SUB, V_CW, V_CB = 0, 8, 12, 13, 13 + CB * CONVW
NCOLP = V_CB + CB


def bc(ap, axis, n):
    a = ap.unsqueeze(axis)
    shape = list(a.shape)
    shape[axis] = n
    return a.broadcast_to(shape)


def block_program(nc, x, w_in, w_out, w_q, keys_t, u, v, rows, ffn_w, cols, consts, out):
    ctx = ExitStack()
    with ctx:
        def sb(name, shape, dt=F32):
            return ctx.enter_context(nc.sbuf_tensor(name, shape, dt))

        def sem(name):
            return ctx.enter_context(nc.semaphore(name))

        X = sb("X", [P, NB, DM])
        Y = sb("Y", [P, NB, DM])
        T8 = sb("T8", [P, KC, SEQ])
        W = sb("W", [P, NHALFW, 4 * HALF])
        XBC = sb("XBC", [P, CB, SEQ + CONVW - 1])
        XC = sb("XC", [P, CB, SEQ])
        MID = sb("MID", [P, 4, NB, HALF])
        Z, Q, K, V = (MID[:, i] for i in range(4))
        QT = sb("QT", [P, DH, SEQ])
        KT = sb("KT", [P, DH, SEQ])
        MIX = sb("MIX", [P, 4 * DM])
        DAB = MIX[:, 0:DM].rearrange("p (h n) -> p h n", n=P)
        SEG = MIX[:, DM:2 * DM].rearrange("p (g n) -> p g n", g=NG)
        PP = MIX[:, 2 * DM:4 * DM].rearrange("p (a j n) -> p a j n", a=2, j=2)
        KEYS = MIX[:, 0:2 * DM].rearrange("p (a n) -> p a n", n=NKEY)
        FW = MIX[:, 2 * DM:3 * DM]
        ROWS = sb("ROWS", [P, NROW])
        COLS = sb("COLS", [P, NCOLP])
        CONST = sb("CONST", [P, NCONST])
        ONES = sb("ONES", [P, P])
        IDENT = CONST[:, C_ID:C_ID + P]
        TRI = CONST[:, C_TRI:C_TRI + P]
        SS = sb("SS", [P, 8 * NB])
        DT = sb("DT", [P, NB, NH])
        DTS = sb("DTS", [P, 6, NB * NH])
        DA = sb("DA", [P, NB, NH])
        ACS = sb("ACS", [P, NB, 2 * NH])
        EACS = sb("EACS", [P, NB, NH])
        DTE = sb("DTE", [P, NB, NH])
        CD = sb("CD", [P, NB, NH])
        AH = sb("AH", [P, NH])
        XS = sb("XS", [P, SSDW])
        BM = sb("BM", [P, NG * NST])
        XDT = sb("XDT", [P, SSDW])
        XDTE = sb("XDTE", [P, SSDW])
        CBM = sb("CBM", [P, NG, P])
        ST = sb("ST", [P, SSDW])
        TMP = sb("TMP", [P, 2, HALF])
        AT = sb("AT", [P, SEQ])
        SMALL = sb("SMALL", [P, 64])
        MX = sb("MX", [P, 2, 2])
        NMX = sb("NMX", [P, 2, 2])
        SUMS = sb("SUMS", [P, 2, 2])
        RS = sb("RS", [P, 2, 2])
        LAM = sb("LAM", [P, 6])
        LT = sb("LT", [P, QKD])
        WC = sb("WC", [P, 8])
        TOPV = sb("TOPV", [P, 2, TOPK])
        TOPI = sb("TOPI", [P, PH, 2, TOPK], U32)
        TOPIF = sb("TOPIF", [P, PH, 2, TOPK])
        TOPS = sb("TOPS", [P, PH, TOPK])
        POS = sb("POS", [P, PH, TOPK], U32)
        PAB = sb("PAB", [P, 2, NSLOT], U32)
        PABF = MIX[:, 4 * DM - 4 * NSLOT:4 * DM - 2 * NSLOT].rearrange("p (j k) -> p j k", j=2)
        ISEL = sb("ISEL", [P, 2, NSLOT])
        G = MIX[:, 3 * DM:3 * DM + NB * NSLOT].rearrange("p (b k) -> p b k", k=NSLOT)
        IDX = sb("IDX", [P, NB, NSLOT], I32)
        IXC = sb("IXC", [P, 2, RING], I32)
        H = MIX[:, 4 * DM - NSLOT:4 * DM]
        GH = MIX[:, 4 * DM - 2 * NSLOT:4 * DM - NSLOT]
        Q2 = [XBC[:, :, 0:SEQ], XC[:, :, :]]
        OH = QT
        CAND = KT[:, 0, 0:TOPK * TOPK]
        ACC = KT[:, 2:4, :]
        SC = MID
        UV = W[:, :, :].rearrange("p a (b n) -> p (a b) n", n=DM)
        PS = [ctx.enter_context(nc.psum_tensor(f"PS{i}", [P, HALF], F32)) for i in range(8)]

        ld_x = [sem(f"ld_x{i}") for i in range(NB)]
        ld_par, ld_keys = sem("ld_par"), sem("ld_keys")
        w_full = [sem(f"w_full{i}") for i in range(NHALFW)]
        sq_done, rs_half, rs_done, y_ready, t_full, t_done = (sem(n) for n in (
            "sq_done", "rs_half", "rs_done", "y_ready", "t_full", "t_done"))
        proj_full, proj_free, conv_done, xc_done = (sem(n) for n in (
            "proj_full", "proj_free", "conv_done", "xc_done"))
        dt_step, dt_act, da_ready = sem("dt_step"), sem("dt_act"), sem("da_ready")
        dab_ready, ssd_in, ssd_in_free, seg_full, seg_ready, seg_exp = (sem(n) for n in (
            "dab_ready", "ssd_in", "ssd_in_free", "seg_full", "seg_ready", "seg_exp"))
        m_ready, xdt_ready, y_full, yoff_full, st_full, y_free, st_ready = (sem(n) for n in (
            "m_ready", "xdt_ready", "y_full", "yoff_full", "st_full", "y_free", "st_ready"))
        qk_ready, qkt_full, qkt_done = sem("qk_ready"), sem("qkt_full"), sem("qkt_done")
        sc_full, mx_ready, exp_done, at_ready, att_full, att_done, pv_full, o_free = (sem(n) for n in (
            "sc_full", "mx_ready", "exp_done", "at_ready", "att_full", "att_done", "pv_full", "o_free"))
        ysq_ready, ysq_done, yrs_half, yrs_done = (sem(n) for n in (
            "ysq_ready", "ysq_done", "yrs_half", "yrs_done"))
        res_full, res_free = sem("res_full"), sem("res_free")
        q2_full, q2_done, ks_full, ks_done = (sem(n) for n in ("q2_full", "q2_done", "ks_full", "ks_done"))
        g_raw, g_exp, idx_ready = sem("g_raw"), sem("g_exp"), sem("idx_ready")
        ixc_ready, used, h_ready, gelu_done, out_ready, stored = (sem(n) for n in (
            "ixc_ready", "used", "h_ready", "gelu_done", "out_ready", "stored"))
        row_in = [sem(f"row_in{i}") for i in range(RING)]
        dve_seq, act_seq, lam_step, lam_act = sem("dve_seq"), sem("act_seq"), sem("lam_step"), sem("lam_act")

        tiles = ([(w_in, COL_XBC), (w_in, COL_XBC + HALF), (w_in, COL_Z), (w_in, COL_Q), (w_in, COL_K),
                  (w_in, COL_V), (w_out, 0), (w_out, HALF)] + [(w_q, i * HALF) for i in range(4)])
        products_of = ([(proj_full, k) for k in (5, 9, 13, 17, 22, 26)] + [(res_full, NB), (res_full, 2 * NB)]
                       + [(q2_full, 4 * (i + 1)) for i in range(4)])
        WDT = TMP[:, 0, 0:KC * NH]

        STEPS = ["S1", "A0", "S2", "A1", "B0", "A2", "B1", "S3", "A3", "B2", "B3", "N"]

        block = ctx.enter_context(nc.Block())

        @block.sync
        def _(sp):
            for b in range(NB):
                sp.dma_start(X[:, b, :], x[b * P:(b + 1) * P, :]).then_inc(ld_x[b], 16)
                if b == 0:
                    sp.dma_start(CONST[:], consts).then_inc(ld_par, 16)
                    sp.dma_start(COLS[:], cols).then_inc(ld_par, 16)
                    sp.dma_start(ROWS[:], rows).then_inc(ld_par, 16)
                    sp.dma_start(WDT.rearrange("p (c n) -> p c n", n=NH),
                                 w_in[:, COL_DT:COL_DT + NH].rearrange("(c p) n -> p c n", p=P)).then_inc(ld_par, 16)
            n = 0
            for mat, c0 in tiles:
                if n == 16:
                    sp.wait_ge(y_ready, 2 * NB)
                    sp.dma_start(KEYS, keys_t).then_inc(ld_keys, 16)
                    sp.dma_start(FW, ffn_w).then_inc(ld_keys, 16)
                for half in range(2):
                    if n >= NHALFW and half == 0:
                        sp.wait_ge(*products_of[n // 2 - 2])
                    src = mat[half * 4 * P:(half + 1) * 4 * P, c0:c0 + HALF].rearrange("(c p) n -> p c n", p=P)
                    sp.dma_start(W[:, n % NHALFW, :].rearrange("p (c n) -> p c n", n=HALF), src)\
                        .then_inc(w_full[n % NHALFW], 16)
                    n += 1
            for b in range(NB):
                sp.wait_ge(out_ready, b + 1)
                sp.dma_start(out[b * P:(b + 1) * P, :], X[:, b, :]).then_inc(stored, 16)
            sp.wait_ge(stored, 16 * NB)

        @block.tensor
        def _(pe):
            tile = [0]

            def transpose_block(kind, b):
                pe.wait_ge(y_ready, kind * NB + b + 1)
                for c in range(2):
                    j = (kind * NB + b) * 2 + c
                    if j >= 4:
                        pe.wait_ge(t_done, j - 3)
                    if kind == 1 and j < 20:
                        pe.wait_ge(y_free, 4 * NB)
                        pe.wait_ge(o_free, NB)
                    for i in range(4):
                        last = nc.tensor.transpose(PS[j % 4][:, i * P:(i + 1) * P],
                                                   Y[:, b, (4 * c + i) * P:(4 * c + i + 1) * P], IDENT)
                    last.then_inc(t_full, 1)

            def weights_in():
                n = tile[0]
                tile[0] += 2
                for half in range(2):
                    pe.wait_ge(w_full[(n + half) % NHALFW], 16 * ((n + half) // NHALFW + 1))
                return n

            job = [0]

            def next_bank():
                j = job[0]
                job[0] += 1
                if j >= 4:
                    pe.wait_ge(proj_free, j - 3)
                return PS[4 + j % 4]

            pe.wait_ge(ld_par, 64)
            for b in range(NB):
                transpose_block(0, b)
            pe.wait_ge(t_done, 2 * NB)

            bank = next_bank()
            for b in range(NB):
                for c in range(KC):
                    last = nc.tensor.matmul(bank[:, b * NH:(b + 1) * NH], T8[:, c, b * P:(b + 1) * P],
                                            WDT[:, c * NH:(c + 1) * NH], start=(c == 0), stop=(c == KC - 1))
            last.then_inc(proj_full, 1)
            for tl in range(2):
                n = weights_in()
                for cb in range(4):
                    bank = next_bank()
                    for c in range(KC):
                        wt = W[:, (n + c // 4) % NHALFW, (c % 4) * HALF + cb * P:(c % 4) * HALF + (cb + 1) * P]
                        last = nc.tensor.matmul(bank[:, :], wt, T8[:, c, :], start=(c == 0), stop=(c == KC - 1))
                    last.then_inc(proj_full, 1)
            for tl in range(4):
                n = weights_in()
                for b in range(NB):
                    bank = next_bank()
                    for c in range(KC):
                        wt = W[:, (n + c // 4) % NHALFW, (c % 4) * HALF:(c % 4 + 1) * HALF]
                        last = nc.tensor.matmul(bank[:, :], T8[:, c, b * P:(b + 1) * P], wt,
                                                start=(c == 0), stop=(c == KC - 1))
                    last.then_inc(proj_full, 1)
                if tl == 1:
                    pe.wait_ge(da_ready, 1)
                    bank = next_bank()
                    for b in range(NB):
                        nc.tensor.matmul(bank[:, b * 16:b * 16 + NH], TRI, DA[:, b, :], start=True, stop=True)
                        last = nc.tensor.matmul(bank[:, b * 16 + NH:b * 16 + 16], ONES[:, :], DA[:, b, :],
                                                start=True, stop=True)
                    last.then_inc(proj_full, 1)
            for i, src in enumerate((Q, K)):
                for b in range(NB):
                    pe.wait_ge(qk_ready, i * NB + b + 1)
                    bank = next_bank()
                    for h in range(DH):
                        last = nc.tensor.transpose(bank[:, h * P:(h + 1) * P], src[:, b, h * P:(h + 1) * P], IDENT)
                    last.then_inc(proj_full, 1)

            pe.wait_ge(proj_free, job[0])
            pe.wait_ge(xc_done, CB)

            def scores(b, h):
                i = b * DH + h
                if i >= 2:
                    pe.wait_ge(exp_done, 2 * (i - 1))
                for j in range(2):
                    last = nc.tensor.matmul(PS[4 + 2 * (i % 2) + j][:, 0:P * (b + 1)],
                                            QT[j * QKD:(j + 1) * QKD, h, b * P:(b + 1) * P],
                                            KT[j * QKD:(j + 1) * QKD, h, 0:P * (b + 1)], start=True, stop=True)
                    last.then_inc(sc_full, 1)

            def values(b, h):
                i = b * DH + h
                pe.wait_ge(at_ready, i + 1)
                if i >= 1:
                    pe.wait_ge(att_done, i)
                for kb in range(b + 1):
                    last = nc.tensor.transpose(PS[3][:, kb * P:(kb + 1) * P],
                                               PP[:, i % 2, 0, kb * P:(kb + 1) * P], IDENT)
                last.then_inc(att_full, 1)
                pe.wait_ge(att_done, i + 1)
                if h == 0:
                    pe.wait_ge(y_free, 4 * b + 2)
                for kb in range(b + 1):
                    last = nc.tensor.matmul(PS[2][:, h * P:(h + 1) * P], AT[:, kb * P:(kb + 1) * P],
                                            V[:, kb, h * P:(h + 1) * P], start=(kb == 0), stop=(kb == b))
                last.then_inc(pv_full, 1)

            for b in range(NB):
                tok = slice(b * P, (b + 1) * P)
                for step in STEPS:
                    if step == "S1":
                        if b:
                            pe.wait_ge(y_free, 4 * b)
                            pe.wait_ge(o_free, b)
                        for i in range(4):
                            last = nc.tensor.transpose(PS[0][:, i * P:(i + 1) * P], XC[:, i, tok], IDENT)
                        last.then_inc(ssd_in, 1)
                        for g in range(NG):
                            nc.tensor.transpose(PS[1][:, g * P:(g + 1) * P], XC[:, 4 + g, tok], IDENT)
                        for g in range(NG):
                            last = nc.tensor.matmul(PS[1][:, (2 + g) * P:(3 + g) * P], XC[:, 4 + g, tok],
                                                    XC[:, 6 + g, tok], start=True, stop=True)
                        last.then_inc(ssd_in, 1)
                        pe.wait_ge(dab_ready, b + 1)
                        for g in range(NG):
                            if g:
                                pe.wait_ge(seg_ready, b * NG + g)
                            for h in range(HPG):
                                last = nc.tensor.matmul(PS[2][:, h * P:(h + 1) * P], DAB[:, g * HPG + h, :], TRI,
                                                        start=True, stop=True)
                            last.then_inc(seg_full, 1)
                    elif step == "S2":
                        pe.wait_ge(m_ready, b * NG + NG)
                        pe.wait_ge(xdt_ready, 2 * b + 1)
                        pe.wait_ge(ssd_in_free, 3 * b + 1)
                        for h in range(NH):
                            last = nc.tensor.matmul(PS[0][:, h * HD:(h + 1) * HD],
                                                    SEG[:, h // HPG, (h % HPG) * P:(h % HPG + 1) * P],
                                                    XDT[:, h * HD:(h + 1) * HD], start=True, stop=True)
                        last.then_inc(y_full, 1)
                        pe.wait_ge(seg_ready, b * NG + NG)
                        if b:
                            pe.wait_ge(st_ready, b)
                            for g in range(NG):
                                last = nc.tensor.matmul(PS[2][:, g * 256:(g + 1) * 256], XC[:, 6 + g, tok],
                                                        ST[:, g * 256:(g + 1) * 256], start=True, stop=True)
                            last.then_inc(yoff_full, 1)
                        pe.wait_ge(ssd_in_free, 3 * b + 3)
                        pe.wait_ge(xdt_ready, 2 * b + 2)
                        for g in range(NG):
                            last = nc.tensor.matmul(PS[1][:, g * 256:(g + 1) * 256], BM[:, g * P:(g + 1) * P],
                                                    XDTE[:, g * 256:(g + 1) * 256], start=True, stop=True)
                        last.then_inc(st_full, 1)
                    elif step[0] == "A":
                        scores(b, int(step[1]))
                    elif step[0] == "B":
                        values(b, int(step[1]))

            for b in range(NB):
                transpose_block(1, b)
            pe.wait_ge(t_done, 4 * NB)
            rj = 0
            for tl in range(2):
                n = weights_in()
                for b in range(NB):
                    if rj >= 4:
                        pe.wait_ge(res_free, rj - 3)
                    else:
                        pe.wait_ge(exp_done, 2 * DH * NB)
                    for c in range(KC):
                        wt = W[:, (n + c // 4) % NHALFW, (c % 4) * HALF:(c % 4 + 1) * HALF]
                        last = nc.tensor.matmul(PS[4 + rj % 4][:, :], T8[:, c, b * P:(b + 1) * P], wt,
                                                start=(c == 0), stop=(c == KC - 1))
                    last.then_inc(res_full, 1)
                    rj += 1
            for b in range(NB):
                transpose_block(2, b)
            pe.wait_ge(t_done, 6 * NB)
            for j in range(2 * PH):
                if j % 4 == 0:
                    n = weights_in()
                if j < 4:
                    pe.wait_ge(res_free, 2 * NB)
                else:
                    pe.wait_ge(q2_done, j - 3)
                for c in range(KC):
                    wt = W[:, (n + c // 4) % NHALFW, (c % 4) * HALF + (j % 4) * P:(c % 4) * HALF + (j % 4 + 1) * P]
                    last = nc.tensor.matmul(PS[4 + j % 4][:, :], wt, T8[:, c, :], start=(c == 0), stop=(c == KC - 1))
                last.then_inc(q2_full, 1)
            pe.wait_ge(q2_done, 2 * PH)
            pe.wait_ge(ld_keys, 32)
            for b in range(NB):
                for c in range(4):
                    j = b * 4 + c
                    if j >= 4:
                        pe.wait_ge(ks_done, j - 3)
                    for i in range(4):
                        hj = 4 * c + i
                        last = nc.tensor.matmul(PS[j % 4][:, i * P:(i + 1) * P],
                                                Q2[hj // 8][:, hj % 8, b * P:(b + 1) * P], KEYS[:, hj, :],
                                                start=True, stop=True)
                    last.then_inc(ks_full, 1)

        @block.scalar
        def _(act):
            seq = [0]

            def sums_of_squares(kind):
                for b in range(NB):
                    if kind == 0:
                        act.wait_ge(ld_x[b], 16)
                    else:
                        act.wait_ge(res_free, NB + b + 1)
                    if kind == 1 and b == 0:
                        act.wait_ge(t_full, 4 * NB)
                    nc.scalar.activation(Y[:, b, :], X[:, b, :], ACT.Square,
                                         accum_out=SS[:, b:b + 1]).then_inc(sq_done, 1)
                act.wait_ge(rs_half, kind + 1)
                nc.scalar.activation(SS[:, 0:NB], SS[:, 0:NB], ACT.Sqrt).then_inc(rs_done, 1)

            sums_of_squares(0)
            job = [0]

            def drain_bank(dst, func=ACT.Copy, view=None):
                j = job[0]
                job[0] += 1
                act.wait_ge(proj_full, j + 1)
                src = PS[4 + j % 4][:, :] if view is None else view(PS[4 + j % 4])
                nc.scalar.activation(dst, src, func).then_inc(proj_free, 1)

            drain_bank(DT[:, :, :].rearrange("p b h -> p (b h)"), view=lambda t: t[:, 0:NB * NH])
            act.wait_ge(dt_step, 1)
            nc.scalar.activation(DTS[:, 1], DTS[:, 0], ACT.Exp, scale=-1.0).then_inc(dt_act, 1)
            act.wait_ge(dt_step, 2)
            nc.scalar.activation(DTS[:, 3], DTS[:, 2], ACT.Ln).then_inc(dt_act, 1)
            nc.scalar.activation(AH[:, :], ROWS[:, R_ALOG:R_ALOG + NH], ACT.Exp).then_inc(dt_act, 1)
            act.wait_ge(lam_step, 2)
            nc.scalar.activation(LAM[:, 2:4], LAM[:, 0:2], ACT.Exp).then_inc(lam_act, 1)
            for cb in range(CB):
                drain_bank(XBC[:, cb, CONVW - 1:])
            for b in range(NB):
                drain_bank(Z[:, b, :], ACT.Silu)
            for cb in range(CB):
                act.wait_ge(conv_done, cb + 1)
                nc.scalar.activation(XC[:, cb, :], XC[:, cb, :], ACT.Silu,
                                     bias=COLS[:, V_CB + cb:V_CB + cb + 1]).then_inc(xc_done, 1)
            for b in range(NB):
                drain_bank(Q[:, b, :])
            drain_bank(ACS[:, :, :].rearrange("p b h -> p (b h)"), view=lambda t: t[:, 0:NB * 2 * NH])
            for dst in (K, V):
                for b in range(NB):
                    drain_bank(dst[:, b, :])
            act.wait_ge(proj_free, 18)
            nc.scalar.activation(EACS[:, :, :], ACS[:, :, 0:NH], ACT.Exp).then_inc(dt_act, 1)
            nc.scalar.activation(CD[:, :, :], ACS[:, :, NH:2 * NH], ACT.Exp).then_inc(dt_act, 1)
            act.wait_ge(dt_step, 3)
            nc.scalar.activation(DTE[:, :, :], DTE[:, :, :], ACT.Exp).then_inc(dt_act, 1)
            for i in range(2):
                act.wait_ge(yrs_half, i + 1)
                nc.scalar.activation(SS[:, 0:8 * NB], SS[:, 0:8 * NB], ACT.Sqrt).then_inc(yrs_done, 1)
            for dst in (QT, KT):
                for b in range(NB):
                    drain_bank(dst[:, :, b * P:(b + 1) * P], view=lambda t: t[:, :].rearrange("p (h n) -> p h n", n=P))

            def exps(b, h):
                i = b * DH + h
                act.wait_ge(mx_ready, i + 1)
                if i >= 2:
                    act.wait_ge(att_full, i - 1)
                for j in range(2):
                    nc.scalar.activation(PP[:, i % 2, j, 0:P * (b + 1)], PS[4 + 2 * (i % 2) + j][:, 0:P * (b + 1)],
                                         ACT.Exp, bias=NMX[:, i % 2, j:j + 1], scale=QKD ** -0.5,
                                         accum_out=SUMS[:, i % 2, j:j + 1]).then_inc(exp_done, 1)

            for b in range(NB):
                for step in STEPS:
                    if step == "S1":
                        if b:
                            act.wait_ge(y_free, 4 * b)
                            act.wait_ge(st_full, b)
                        act.wait_ge(ssd_in, 2 * b + 1)
                        nc.scalar.activation(XS[:, :], PS[0][:, :], ACT.Copy).then_inc(ssd_in_free, 1)
                        act.wait_ge(ssd_in, 2 * b + 2)
                        nc.scalar.activation(BM[:, :], PS[1][:, 0:NG * P], ACT.Copy).then_inc(ssd_in_free, 1)
                        for g in range(NG):
                            act.wait_ge(seg_ready, b * NG + g + 1)
                            nc.scalar.activation(SEG[:, g, :], SEG[:, g, :], ACT.Exp).then_inc(seg_exp, 1)
                    elif step[0] == "A":
                        exps(b, int(step[1]))
                    elif step[0] == "B":
                        i = b * DH + int(step[1])
                        act.wait_ge(att_full, i + 1)
                        if i:
                            act.wait_ge(pv_full, i)
                        nc.scalar.activation(AT[:, 0:P * (b + 1)], PS[3][:, 0:P * (b + 1)], ACT.Copy)\
                            .then_inc(att_done, 1)
                    elif step == "N":
                        act.wait_ge(yrs_half, 2 + b + 1)
                        nc.scalar.activation(SMALL[:, 0:6], SMALL[:, 0:6], ACT.Sqrt).then_inc(yrs_done, 1)

            sums_of_squares(1)
            for j in range(2 * PH):
                act.wait_ge(q2_full, j + 1)
                nc.scalar.activation(Q2[j // 8][:, j % 8, :], PS[4 + j % 4][:, :], ACT.Copy).then_inc(q2_done, 1)
            for j in range(4 * NB):
                act.wait_ge(ks_full, j + 1)
                nc.scalar.activation(SC[:, j // 4, j % 4, :], PS[j % 4][:, :], ACT.Copy).then_inc(ks_done, 1)
            for b in range(NB):
                act.wait_ge(g_raw, b + 1)
                nc.scalar.activation(G[:, b, :], G[:, b, :], ACT.Exp).then_inc(g_exp, 1)
                act.wait_ge(h_ready, b + 1)
                nc.scalar.activation(H[:, :], H[:, :], ACT.Gelu).then_inc(gelu_done, 1)

        @block.vector
        def _(dve):
            seq = [0]

            def link(ins):
                seq[0] += 1
                ins.then_inc(dve_seq, 1)
                dve.wait_ge(dve_seq, seq[0])

            tt, ts, stt = nc.vector.tensor_tensor, nc.vector.tensor_scalar, nc.vector.scalar_tensor_tensor

            def inverse_mean(dst, src, n):
                link(ts(dst, src, 1.0 / n, EPS, ALU.mult, ALU.add))
                return nc.vector.reciprocal(dst, dst)

            def evacuate_transposes(kind):
                for b in range(NB):
                    for c in range(2):
                        j = (kind * NB + b) * 2 + c
                        dve.wait_ge(t_full, j + 1)
                        src = PS[j % 4][:, :].rearrange("p (i n) -> p i n", n=P)
                        dst = T8[:, 4 * c:4 * c + 4, b * P:(b + 1) * P]
                        if kind == 0:
                            w = COLS[:, V_MIX + 4 * c:V_MIX + 4 * c + 4]
                            tt(dst, src, bc(w, 2, P), ALU.mult).then_inc(t_done, 1)
                        elif kind == 1:
                            tt(dst, src, bc(WC[:, 4 * c:4 * c + 4], 2, P), ALU.mult).then_inc(t_done, 1)
                        else:
                            nc.vector.tensor_copy(dst, src).then_inc(t_done, 1)

            nc.vector.memset(ONES[:, :], 1.0)
            nc.vector.memset(XBC[:, :, 0:CONVW - 1], 0.0)
            link(nc.vector.memset(ST[:, :], 0.0))
            dve.wait_ge(ld_par, 64)
            nc.vector.tensor_copy(WC[:, 0:4], COLS[:, V_SSD:V_SSD + 4])
            link(ts(WC[:, 4:8], COLS[:, V_SUB:V_SUB + 1].broadcast_to([P, 4]), 1.0 - LAMBDA_INIT, None, ALU.mult))
            dve.wait_ge(sq_done, NB)
            inverse_mean(SS[:, 0:NB], SS[:, 0:NB], DM).then_inc(rs_half, 1)
            dve.wait_ge(rs_done, 1)
            for b in range(NB):
                ts(Y[:, b, :], X[:, b, :], SS[:, b:b + 1], None, ALU.mult).then_inc(y_ready, 1)
            evacuate_transposes(0)

            dt = DT[:, :, :].rearrange("p b h -> p (b h)")
            dve.wait_ge(proj_free, 1)
            link(tt(DT[:, :, :], DT[:, :, :], bc(ROWS[:, R_DTB:R_DTB + NH], 1, NB), ALU.add))
            stt(DTS[:, 0], dt, -1.0, dt, ALU.mult, ALU.max).then_inc(dt_step, 1)
            dve.wait_ge(dt_act, 1)
            ts(DTS[:, 2], DTS[:, 1], 1.0, None, ALU.add).then_inc(dt_step, 1)
            dve.wait_ge(dt_act, 2)
            link(ts(DTS[:, 4], DTS[:, 2], 1.0, None, ALU.is_equal))
            link(tt(DTS[:, 3], DTS[:, 3], DTS[:, 4], ALU.add))
            link(stt(DTS[:, 5], DTS[:, 2], -1.0, DTS[:, 4], ALU.add, ALU.add))
            link(nc.vector.reciprocal(DTS[:, 5], DTS[:, 5]))
            link(tt(DTS[:, 3], DTS[:, 3], DTS[:, 5], ALU.mult))
            link(tt(DTS[:, 3], DTS[:, 3], DTS[:, 1], ALU.mult))
            link(stt(dt, dt, 0.0, DTS[:, 3], ALU.max, ALU.add))
            dve.wait_ge(dt_act, 3)
            stt(DA[:, :, :], DT[:, :, :], -1.0, bc(AH[:, :], 1, NB), ALU.mult, ALU.mult).then_inc(da_ready, 1)
            for i in range(2):
                a = ROWS[:, R_L + 128 * i:R_L + 128 * i + QKD]
                c = ROWS[:, R_L + 128 * i + QKD:R_L + 128 * i + 128]
                link(stt(LT[:, :], a, 1.0, c, ALU.mult, ALU.mult))
                nc.vector.reduce_sum(LAM[:, i:i + 1], LT[:, :], AXX).then_inc(lam_step, 1)
                dve.wait_ge(lam_step, i + 1)
            dve.wait_ge(lam_act, 1)
            link(tt(LAM[:, 4:5], LAM[:, 2:3], LAM[:, 3:4], ALU.subtract))
            link(ts(LAM[:, 4:5], LAM[:, 4:5], LAMBDA_INIT, -1.0, ALU.add, ALU.mult))

            for cb in range(CB):
                dve.wait_ge(proj_free, 2 + cb)
                w = lambda k: COLS[:, V_CW + cb * CONVW + k:V_CW + cb * CONVW + k + 1]
                link(ts(XC[:, cb, :], XBC[:, cb, 0:SEQ], w(0), None, ALU.mult))
                for k in range(1, CONVW):
                    ins = stt(XC[:, cb, :], XBC[:, cb, k:k + SEQ], w(k), XC[:, cb, :], ALU.mult, ALU.add)
                    if k < CONVW - 1:
                        link(ins)
                ins.then_inc(conv_done, 1)

            for i, (src, first) in enumerate(((Q, 14), (K, 19))):
                nw = ROWS[:, (R_QN, R_KN)[i]:(R_QN, R_KN)[i] + QKD]
                for b in range(NB):
                    dve.wait_ge(proj_free, first + b)
                    link(tt(TMP[:, 0, :], src[:, b, :], src[:, b, :], ALU.mult))
                    link(nc.vector.reduce_sum(SS[:, 8 * b:8 * b + 8],
                                              TMP[:, 0, :].rearrange("p (g d) -> p g d", d=QKD), AXX))
                inverse_mean(SS[:, 0:8 * NB], SS[:, 0:8 * NB], QKD).then_inc(yrs_half, 1)
                if i == 0:
                    dve.wait_ge(proj_free, 18)
                    tt(DTE[:, :, :], ACS[:, :, NH:2 * NH], ACS[:, :, 0:NH], ALU.subtract).then_inc(dt_step, 1)
                dve.wait_ge(yrs_done, i + 1)
                for b in range(NB):
                    h3 = src[:, b, :].rearrange("p (g d) -> p g d", d=QKD)
                    link(tt(h3, h3, bc(SS[:, 8 * b:8 * b + 8], 2, QKD), ALU.mult))
                    link(tt(h3, h3, bc(nw, 1, 8), ALU.mult))
                    cos = bc(CONST[:, C_COS + b * RD:C_COS + (b + 1) * RD], 1, 8)
                    sin = bc(CONST[:, C_SIN + b * RD:C_SIN + (b + 1) * RD], 1, 8)
                    t = [TMP[:, 1, 64 * k:64 * k + 64].rearrange("p (g d) -> p g d", d=RD) for k in range(4)]
                    tt(t[0], h3[:, :, 0:RD], cos, ALU.mult)
                    tt(t[1], h3[:, :, RD:2 * RD], sin, ALU.mult)
                    tt(t[2], h3[:, :, 0:RD], sin, ALU.mult)
                    link(tt(t[3], h3[:, :, RD:2 * RD], cos, ALU.mult))
                    tt(h3[:, :, 0:RD], t[0], t[1], ALU.subtract)
                    tt(h3[:, :, RD:2 * RD], t[2], t[3], ALU.add).then_inc(qk_ready, 1)
                    dve.wait_ge(qk_ready, i * NB + b + 1)

            hd3 = lambda ap: ap.rearrange("p (h d) -> p h d", d=HD)
            for b in range(NB):
                i0 = b * DH
                for step in STEPS:
                    if step == "S1":
                        if b:
                            dve.wait_ge(seg_full, NG * b)
                            dve.wait_ge(st_full, b)
                        nc.vector.tensor_copy(DAB[:, :, :], bc(DA[:, b, :], 2, P)).then_inc(dab_ready, 1)
                        for g in range(NG):
                            dve.wait_ge(seg_full, NG * b + g + 1)
                            for h in range(HPG):
                                hh = g * HPG + h
                                last = ts(SEG[:, g, h * P:(h + 1) * P], PS[2][:, h * P:(h + 1) * P],
                                          ACS[:, b, hh:hh + 1], 0.0, ALU.subtract, ALU.min)
                            last.then_inc(seg_ready, 1)
                        dve.wait_ge(ssd_in_free, 3 * b + 2)
                        tt(CBM[:, :, :], PS[1][:, NG * P:2 * NG * P].rearrange("p (g n) -> p g n", n=P),
                           bc(TRI, 1, NG), ALU.mult).then_inc(ssd_in_free, 1)
                        dve.wait_ge(ssd_in_free, 3 * b + 3)
                        tt(hd3(XDT[:, :]), hd3(XS[:, :]), bc(DT[:, b, :], 2, HD), ALU.mult).then_inc(xdt_ready, 1)
                        dve.wait_ge(xdt_ready, 2 * b + 1)
                        dve.wait_ge(dt_act, 6)
                        tt(hd3(XDTE[:, :]), hd3(XDT[:, :]), bc(DTE[:, b, :], 2, HD), ALU.mult).then_inc(xdt_ready, 1)
                        for g in range(NG):
                            dve.wait_ge(seg_exp, NG * b + g + 1)
                            m = SEG[:, g, :].rearrange("p (h n) -> p h n", n=P)
                            tt(m, m, bc(CBM[:, g, :], 1, HPG), ALU.mult).then_inc(m_ready, 1)
                    elif step == "S2":
                        y = Y[:, b, 0:SSDW]
                        link(tt(hd3(y), hd3(XS[:, :]), bc(ROWS[:, R_D:R_D + NH], 2, HD), ALU.mult))
                        dve.wait_ge(y_full, b + 1)
                        tt(y, y, PS[0][:, :], ALU.add).then_inc(y_free, 1)
                        dve.wait_ge(y_free, 4 * b + 1)
                        if b:
                            dve.wait_ge(yoff_full, b)
                            link(tt(hd3(TMP[:, 0, :]), hd3(PS[2][:, :]), bc(EACS[:, b, :], 2, HD), ALU.mult))
                            tt(y, y, TMP[:, 0, :], ALU.add).then_inc(y_free, 1)
                        else:
                            nc.vector.tensor_copy(TMP[:, 0, 0:2], TMP[:, 0, 2:4]).then_inc(y_free, 1)
                        dve.wait_ge(y_free, 4 * b + 2)
                    elif step == "S3":
                        dve.wait_ge(st_full, b + 1)
                        link(tt(hd3(ST[:, :]), hd3(ST[:, :]), bc(CD[:, b, :], 2, HD), ALU.mult))
                        tt(ST[:, :], ST[:, :], PS[1][:, :], ALU.add).then_inc(st_ready, 1)
                        dve.wait_ge(st_ready, b + 1)
                        y = Y[:, b, 0:SSDW]
                        link(tt(y, y, Z[:, b, :], ALU.mult))
                        tt(TMP[:, 0, :], y, y, ALU.mult).then_inc(y_free, 1)
                        dve.wait_ge(y_free, 4 * b + 3)
                        nc.vector.reduce_sum(SMALL[:, 0:NG], TMP[:, 0, :].rearrange("p (g d) -> p g d", g=NG), AXX)\
                            .then_inc(y_free, 1)
                        dve.wait_ge(y_free, 4 * b + 4)
                    elif step[0] == "A":
                        i = i0 + int(step[1])
                        for j in range(2):
                            bank = PS[4 + 2 * (i % 2) + j]
                            dve.wait_ge(sc_full, 2 * i + j + 1)
                            link(nc.vector.memset(bank[0:64, b * P + 64:(b + 1) * P], NEG))
                            link(nc.vector.reduce_max(MX[:, i % 2, j:j + 1], bank[:, 0:P * (b + 1)], AXX))
                        if i >= 2:
                            dve.wait_ge(exp_done, 2 * (i - 1))
                        ts(NMX[:, i % 2, :], MX[:, i % 2, :], -(QKD ** -0.5), None, ALU.mult).then_inc(mx_ready, 1)
                        dve.wait_ge(mx_ready, i + 1)
                    elif step[0] == "B":
                        i = i0 + int(step[1])
                        n = P * (b + 1)
                        dve.wait_ge(exp_done, 2 * i + 2)
                        link(nc.vector.reciprocal(RS[:, i % 2, :], SUMS[:, i % 2, :]))
                        link(ts(RS[:, i % 2, 1:2], RS[:, i % 2, 1:2], LAM[:, 4:5], None, ALU.mult))
                        link(ts(PP[:, i % 2, 1, 0:n], PP[:, i % 2, 1, 0:n], RS[:, i % 2, 1:2], None, ALU.mult))
                        stt(PP[:, i % 2, 0, 0:n], PP[:, i % 2, 0, 0:n], RS[:, i % 2, 0:1], PP[:, i % 2, 1, 0:n],
                            ALU.mult, ALU.add).then_inc(at_ready, 1)
                        dve.wait_ge(at_ready, i + 1)
                    elif step == "N":
                        dve.wait_ge(pv_full, DH * (b + 1))
                        yd = Y[:, b, SSDW:DM]
                        nc.vector.tensor_copy(yd, PS[2][:, :]).then_inc(o_free, 1)
                        dve.wait_ge(o_free, b + 1)
                        link(tt(TMP[:, 1, :], yd, yd, ALU.mult))
                        link(nc.vector.reduce_sum(SMALL[:, 2:6], TMP[:, 1, :].rearrange("p (g d) -> p g d", d=VD), AXX))
                        ts(SMALL[:, 0:2], SMALL[:, 0:2], 1.0 / 256, EPS, ALU.mult, ALU.add)
                        link(ts(SMALL[:, 2:6], SMALL[:, 2:6], 1.0 / VD, EPS, ALU.mult, ALU.add))
                        nc.vector.reciprocal(SMALL[:, 0:6], SMALL[:, 0:6]).then_inc(yrs_half, 1)
                        dve.wait_ge(yrs_done, 2 + b + 1)
                        y3 = Y[:, b, 0:SSDW].rearrange("p (g d) -> p g d", g=NG)
                        tt(y3, y3, bc(SMALL[:, 0:2], 2, 256), ALU.mult)
                        y3 = yd.rearrange("p (g d) -> p g d", d=VD)
                        tt(y3, y3, bc(SMALL[:, 2:6], 2, VD), ALU.mult).then_inc(y_ready, 1)
                        dve.wait_ge(y_ready, NB + b + 1)

            evacuate_transposes(1)
            rj = 0
            for tl in range(2):
                for b in range(NB):
                    dve.wait_ge(res_full, rj + 1)
                    xb = X[:, b, tl * HALF:(tl + 1) * HALF]
                    tt(xb, xb, PS[4 + rj % 4][:, :], ALU.add).then_inc(res_free, 1)
                    rj += 1
            dve.wait_ge(sq_done, 2 * NB)
            inverse_mean(SS[:, 0:NB], SS[:, 0:NB], DM).then_inc(rs_half, 1)
            dve.wait_ge(rs_done, 2)
            dve.wait_ge(ld_keys, 32)
            for b in range(NB):
                stt(Y[:, b, :], X[:, b, :], SS[:, b:b + 1], FW[:, :], ALU.mult, ALU.mult).then_inc(y_ready, 1)
            evacuate_transposes(2)

            def top16(vals, values, places):
                link(nc.vector.max(values[:, 0:8], vals))
                nc.vector.max_index(places[:, 0:8], values[:, 0:8], vals)
                link(nc.vector.match_replace(vals, values[:, 0:8], vals, NEG))
                link(nc.vector.max(values[:, 8:16], vals))
                link(nc.vector.max_index(places[:, 8:16], values[:, 8:16], vals))

            def route(b):
                dve.wait_ge(ks_done, 4 * b + 4)
                sc = SC[:, b, :, :].rearrange("p a (i n) -> p (a i) n", n=NKEY)
                for h in range(PH):
                    for j in range(2):
                        top16(sc[:, 2 * h + j, :], TOPV[:, j, :], TOPI[:, h, j, :])
                    link(tt(CAND.rearrange("p (a c) -> p a c", c=TOPK), bc(TOPV[:, 0, :], 2, TOPK),
                            bc(TOPV[:, 1, :], 1, TOPK), ALU.add))
                    top16(CAND, TOPS[:, h, :], POS[:, h, :])
                tt(G[:, b, :].rearrange("p (h k) -> p h k", k=TOPK), TOPS[:, :, :],
                   TOPS[:, :, 0:1].broadcast_to([P, PH, TOPK]), ALU.subtract).then_inc(g_raw, 1)
                pos = POS[:, :, :].rearrange("p h k -> p (h k)")
                ts(PAB[:, 0, :], pos, 4, None, ALU.logical_shift_right)
                link(ts(PAB[:, 1, :], pos, 15, None, ALU.bitwise_and))
                nc.vector.tensor_copy(PABF[:, :, :], PAB[:, :, :])
                link(nc.vector.tensor_copy(TOPIF[:, :, :, :], TOPI[:, :, :, :]))
                for j in range(2):
                    for q in range(4):
                        oh = OH[:, q, :].rearrange("p (k c) -> p k c", c=TOPK)
                        ph = PABF[:, j, 32 * q:32 * q + 32]
                        link(tt(oh, bc(CONST[:, C_IOTA:C_IOTA + TOPK], 1, 32), bc(ph, 2, TOPK), ALU.is_equal))
                        for h2 in range(2):
                            o = OH[:, q, h2 * 256:(h2 + 1) * 256].rearrange("p (k c) -> p k c", c=TOPK)
                            link(tt(o, o, bc(TOPIF[:, 2 * q + h2, j, :], 1, TOPK), ALU.mult))
                        link(nc.vector.reduce_sum(ISEL[:, j, 32 * q:32 * q + 32], oh, AXX))
                stt(IDX[:, b, :], ISEL[:, 0, :], float(NKEY), ISEL[:, 1, :], ALU.mult, ALU.add).then_inc(idx_ready, 1)
                dve.wait_ge(idx_ready, b + 1)
                dve.wait_ge(g_exp, b + 1)
                g3 = G[:, b, :].rearrange("p (h k) -> p h k", k=TOPK)
                link(nc.vector.reduce_sum(SMALL[:, 8:16], g3, AXX))
                link(nc.vector.reciprocal(SMALL[:, 8:16], SMALL[:, 8:16]))
                link(tt(g3, g3, bc(SMALL[:, 8:16], 2, TOPK), ALU.mult))

            for b in range(NB):
                route(b)
                slot0 = 2 * NSLOT * b
                acc1 = ACC.rearrange("p a n -> p (a n)")
                link(nc.vector.memset(ACC, 0.0))
                with dve.Fori(0, NSLOT // RING, 1) as it:
                    for r in range(RING):
                        dve.wait_ge(row_in[r], it * 16 + (16 * (2 * b * NSLOT // RING + 1)))
                        stt(UV[:, r, :], UV[:, r, :], 1.0, Y[:, b, :], ALU.mult, ALU.mult,
                            accum_out=H[:, bass.ds(it * RING + r, 1)]).then_inc(used, 1)
                dve.wait_ge(used, slot0 + NSLOT)
                nc.vector.tensor_copy(GH[:, :], H[:, :]).then_inc(h_ready, 1)
                dve.wait_ge(gelu_done, b + 1)
                link(tt(GH[:, :], G[:, b, :], H[:, :], ALU.mult))
                with dve.Fori(0, NSLOT // RING, 1) as it:
                    for r in range(RING):
                        dve.wait_ge(row_in[r], it * 16 + (16 * ((2 * b + 1) * NSLOT // RING + 1)))
                        dve.wait_ge(used, it * RING + (slot0 + NSLOT + r - 1))
                        acc = X[:, b, :] if r % 2 == 0 else acc1
                        stt(acc, UV[:, r, :], GH[:, bass.ds(it * RING + r, 1)], acc, ALU.mult, ALU.add)\
                            .then_inc(used, 1)
                dve.wait_ge(used, slot0 + 2 * NSLOT)
                tt(X[:, b, :], X[:, b, :], acc1, ALU.add).then_inc(out_ready, 1)
                dve.wait_ge(out_ready, b + 1)

        @block.gpsimd
        def _(pool):
            pool.wait_ge(q2_full, 2 * PH)

            def fetch(b, table, group, it, first):
                for half in range(2):
                    nc.gpsimd.tensor_copy(IXC[:, half, :], IDX[:, b, bass.ds(it * (2 * RING) + half * RING, RING)])\
                        .then_inc(ixc_ready, 1)
                    pool.wait_ge(ixc_ready, it * 2 + (group + half + 1))
                    for r in range(RING):
                        if half or not first:
                            pool.wait_ge(used, use)
                            pool.reg_add(use, use, 1)
                        pool.indirect_dma_start(UV[:, r, :], None, table,
                                                bass.IndirectOffsetOnAxis(IXC[:, half, r:r + 1], 0))\
                            .then_inc(row_in[r], 16)

            use = pool.alloc_register("use")
            pool.reg_mov(use, 1)
            group = 0
            for b in range(NB):
                pool.wait_ge(idx_ready, b + 1)
                for table in (u, v):
                    start = 1 if group == 0 else 0
                    if start:
                        fetch(b, table, group, 0, True)
                    with pool.Fori(start, NSLOT // (2 * RING), 1) as it:
                        fetch(b, table, group, it, False)
                    group += NSLOT // RING


def kernel(**inputs):
    import concourse.bacc as bacc
    from concourse.bass_utils import run_bass_kernel_spmd as run

    f = {k: np.asarray(a) for k, a in inputs.items()}
    vec = lambda name: f[name].reshape(-1)
    rows = np.concatenate([vec(n) for n in ("dt_bias", "a_log", "d_skip", "q_norm_w", "k_norm_w",
                                            "lambda_q1", "lambda_k1", "lambda_q2", "lambda_k2")])
    cols = np.concatenate([
        vec("mix_norm_w").reshape(8, P).T, vec("ssd_norm_w").reshape(4, P).T, vec("subln_w").reshape(1, P).T,
        f["conv_w"][0].T.reshape(CB, P, CONVW).transpose(1, 0, 2).reshape(P, CB * CONVW),
        vec("conv_b").reshape(CB, P).T], axis=1)
    inv = np.power(np.float32(500000.0), -np.arange(0, 16, 2, dtype=np.float32) / np.float32(16))
    ang = np.arange(SEQ, dtype=np.float32)[:, None] * inv[None, :].astype(np.float32)
    table = lambda t: t.astype(np.float32).reshape(NB, P, RD).transpose(1, 0, 2).reshape(P, NB * RD)
    consts = np.concatenate([np.eye(P, dtype=np.float32), np.triu(np.ones((P, P), np.float32)),
                             table(np.cos(ang)), table(np.sin(ang)),
                             np.broadcast_to(np.arange(16, dtype=np.float32), (P, 16))], axis=1)
    arrays = {
        "x": f["x"][0], "w_in": f["w_in"][0], "w_out": f["w_out"][0], "w_q": f["peer_w_q"][0],
        "keys_t": f["peer_sub_keys"][0].reshape(2 * PH, NKEY, P).transpose(2, 0, 1),
        "u": f["peer_u"][0], "v": f["peer_v"][0], "rows": np.broadcast_to(rows, (P, NROW)),
        "ffn_w": np.broadcast_to(vec("ffn_norm_w"), (P, DM)), "cols": cols, "consts": consts,
    }
    arrays = {k: np.ascontiguousarray(a) for k, a in arrays.items()}
    nc = bacc.Bacc("TRN2", target_bir_lowering=False, num_devices=1)
    args = [nc.dram_tensor(k, a.shape, F32, kind="ExternalInput").ap() for k, a in arrays.items()]
    args.append(nc.dram_tensor("out", (SEQ, DM), F32, kind="ExternalOutput").ap())
    block_program(nc, *args)
    r = run(nc, [arrays], core_ids=[0])
    return r.results[0]["out"].reshape(1, SEQ, DM)
```

```python
import math
import numpy as np
import concourse.bass as bass
from concourse import mybir
from contextlib import ExitStack

F32 = mybir.dt.float32
I32 = mybir.dt.int32
U32 = mybir.dt.uint32
ALU = mybir.AluOpType
ACT = mybir.ActivationFunctionType
AXX = mybir.AxisListType.X

P = 128
SEQ, DM = 512, 1024
NB = SEQ // P
KC = DM // P
HALF = 512
SSDW, HD, NH, NG, NST = 512, 64, 8, 2, 128
HPG = NH // NG
CONVW, CONVC = 4, 1024
CB = CONVC // P
DH, QKD, VD = 4, 64, 128
RD = 8
EPS = 1e-6
LAMBDA_INIT = 0.8 - 0.6 * math.exp(-0.3 * 0)
PH, TOPK, NKEY, NEXP = 8, 16, 128, 128 * 128
NSLOT = PH * TOPK
NEG = -3.0e38
NHALFW = 4
RING = 4
STEP = 8
NG_TOK = 4
HB = NB // 2
HT = HB * P
COL_Z, COL_XBC, COL_DT, COL_Q, COL_K, COL_V = 0, 512, 1536, 1544, 2056, 2568

R_DTB, R_ALOG, R_D, R_QN, R_KN, R_L = 0, 8, 16, 24, 88, 152
NROW = R_L + 4 * 64
C_ID, C_TRI, C_COS, C_SIN, C_IOTA = 0, 128, 256, 256 + NB * RD, 256 + 2 * NB * RD
NCONST = C_IOTA + NKEY
V_MIX, V_SSD, V_SUB, V_CW, V_CB = 0, 8, 12, 13, 13 + CB * CONVW
NCOLP = V_CB + CB


def bc(ap, axis, n):
    a = ap.unsqueeze(axis)
    shape = list(a.shape)
    shape[axis] = n
    return a.broadcast_to(shape)


def block_program(nc, x, w_in, w_out, w_q, keys_t, u, u_t, v, rows, ffn_w, cols, consts, out):
    ctx = ExitStack()
    with ctx:
        def sb(name, shape, dt=F32):
            return ctx.enter_context(nc.sbuf_tensor(name, shape, dt))

        def sem(name):
            return ctx.enter_context(nc.semaphore(name))

        X = sb("X", [P, NB, DM])
        Y = sb("Y", [P, NB, DM])
        T8 = sb("T8", [P, 2, KC, HT])
        BIG = sb("BIG", [P, 32832])
        place = [0]

        def part(n):
            place[0] += n
            return BIG[:, place[0] - n:place[0]]

        W = part(NHALFW * 4 * HALF).rearrange("p (a n) -> p a n", a=NHALFW)
        XBC = part(CB * (SEQ + CONVW - 1)).rearrange("p (c n) -> p c n", c=CB)
        XC = part(CB * SEQ).rearrange("p (c n) -> p c n", c=CB)
        MID = part(4 * NB * HALF).rearrange("p (a b n) -> p a b n", a=4, b=NB)
        Z, Q, K, V = (MID[:, i] for i in range(4))
        QT = part(DH * SEQ).rearrange("p (h n) -> p h n", h=DH)
        KT = part(DH * SEQ).rearrange("p (h n) -> p h n", h=DH)
        MIX = part(4 * DM)
        DAB = MIX[:, 0:DM].rearrange("p (h n) -> p h n", n=P)
        SEG = MIX[:, DM:2 * DM].rearrange("p (g n) -> p g n", g=NG)
        PP = MIX[:, 2 * DM:4 * DM].rearrange("p (a j n) -> p a j n", a=2, j=2)
        GD = BIG[:, 0:HT * NKEY].rearrange("p (t j) -> p t j", j=NKEY)
        KEYS = MIX[:, 0:2 * DM].rearrange("p (a n) -> p a n", n=NKEY)
        FW = MIX[:, 2 * DM:3 * DM]
        ROWS = sb("ROWS", [P, NROW])
        COLS = sb("COLS", [P, NCOLP])
        CONST = sb("CONST", [P, NCONST])
        ONES = sb("ONES", [P, P])
        IDENT = CONST[:, C_ID:C_ID + P]
        TRI = CONST[:, C_TRI:C_TRI + P]
        SS = sb("SS", [P, 8 * NB])
        DT = sb("DT", [P, NB, NH])
        DTS = sb("DTS", [P, 6, NB * NH])
        DA = sb("DA", [P, NB, NH])
        ACS = sb("ACS", [P, NB, 2 * NH])
        EACS = sb("EACS", [P, NB, NH])
        DTE = sb("DTE", [P, NB, NH])
        CD = sb("CD", [P, NB, NH])
        AH = sb("AH", [P, NH])
        UV = sb("UV", [P, RING, DM])
        XS, XDT, XDTE = UV[:, 0, 0:SSDW], UV[:, 0, SSDW:DM], UV[:, 1, 0:SSDW]
        ST = UV[:, 1, SSDW:DM]
        TMP = UV[:, 2, :].rearrange("p (a n) -> p a n", a=2)
        AT, BM = UV[:, 3, 0:SEQ], UV[:, 3, SEQ:SEQ + NG * NST]
        CBM = UV[:, 3, SEQ + 256:DM].rearrange("p (g n) -> p g n", g=NG)
        SMALL = sb("SMALL", [P, 64])
        MX = sb("MX", [P, 2, 2])
        NMX = sb("NMX", [P, 2, 2])
        SUMS = sb("SUMS", [P, 2, 2])
        RS = sb("RS", [P, 2, 2])
        LAM = sb("LAM", [P, 6])
        LT = sb("LT", [P, QKD])
        WC = sb("WC", [P, 8])
        TOPV = KT[:, 3, 0:32].rearrange("p (j k) -> p j k", j=2)
        TOPS = KT[:, 3, 32:160].rearrange("p (h k) -> p h k", k=TOPK)
        TOPIF = KT[:, 3, 160:416].rearrange("p (h j k) -> p h j k", j=2, k=TOPK)
        TOPI = MIX[:, 3 * DM:3 * DM + 256].bitcast(U32).rearrange("p (h j k) -> p h j k", j=2, k=TOPK)
        POS = MIX[:, 3 * DM + 256:3 * DM + 384].bitcast(U32).rearrange("p (h k) -> p h k", k=TOPK)
        PAB = MIX[:, 3 * DM + 384:3 * DM + 640].bitcast(U32).rearrange("p (j k) -> p j k", j=2)
        PABF = MIX[:, 3 * DM + 640:3 * DM + 896].rearrange("p (j k) -> p j k", j=2)
        ISELS = KT[:, 1:3, :].rearrange("p a (b j k) -> p (a b) j k", b=2, j=2)
        G = sb("G", [P, NB, NSLOT])
        IDX = sb("IDX", [P, HB, NSLOT], I32)
        IXC = sb("IXC", [P, 2, STEP], I32)
        H = sb("H", [P, NSLOT])
        GH = sb("GH", [P, NSLOT])
        KT3 = sb("KT3", [P, 3, HT])
        GE = sb("GE", [P, 2, HT])
        ONEHOT = Y[:, HB:NB, :].rearrange("p b (i a k) -> p b i a k", i=NG_TOK, a=2)
        UT = T8[:, 0, :, :].rearrange("p (q c) (h i) -> p q (c h) i", q=2, h=2)
        VT = Y[:, HB:NB, :]
        Q2 = [XBC[:, :, 0:SEQ], XC[:, :, :]]
        OH = QT
        CAND = KT[:, 0, 0:TOPK * TOPK]
        SC = MID
        PS = [ctx.enter_context(nc.psum_tensor(f"PS{i}", [P, HALF], F32)) for i in range(8)]

        ld_x = [sem(f"ld_x{i}") for i in range(NB)]
        ld_par, ld_keys = sem("ld_par"), sem("ld_keys")
        w_full = [sem(f"w_full{i}") for i in range(NHALFW)]
        sq_done, rs_half, rs_done, y_ready, t_full, t_done = (sem(n) for n in (
            "sq_done", "rs_half", "rs_done", "y_ready", "t_full", "t_done"))
        proj_full, proj_free, conv_done, xc_done = (sem(n) for n in (
            "proj_full", "proj_free", "conv_done", "xc_done"))
        dt_step, dt_act, da_ready = sem("dt_step"), sem("dt_act"), sem("da_ready")
        dab_ready, ssd_in, ssd_in_free, seg_full, seg_ready, seg_exp = (sem(n) for n in (
            "dab_ready", "ssd_in", "ssd_in_free", "seg_full", "seg_ready", "seg_exp"))
        m_ready, xdt_ready, y_full, yoff_full, st_full, y_free, st_ready = (sem(n) for n in (
            "m_ready", "xdt_ready", "y_full", "yoff_full", "st_full", "y_free", "st_ready"))
        qk_ready, qkt_full, qkt_done = sem("qk_ready"), sem("qkt_full"), sem("qkt_done")
        sc_full, mx_ready, exp_done, at_ready, att_full, att_done, pv_full, o_free = (sem(n) for n in (
            "sc_full", "mx_ready", "exp_done", "at_ready", "att_full", "att_done", "pv_full", "o_free"))
        ysq_ready, ysq_done, yrs_half, yrs_done = (sem(n) for n in (
            "ysq_ready", "ysq_done", "yrs_half", "yrs_done"))
        res_full, res_free = sem("res_full"), sem("res_free")
        q2_full, q2_done, ks_full, ks_done = (sem(n) for n in ("q2_full", "q2_done", "ks_full", "ks_done"))
        g_raw, g_exp, idx_ready = sem("g_raw"), sem("g_exp"), sem("idx_ready")
        ixc_ready, used, h_ready, gelu_done, out_ready, stored = (sem(n) for n in (
            "ixc_ready", "used", "h_ready", "gelu_done", "out_ready", "stored"))
        sel_ready, selt_full, selt_done, oh_ready, gb_full, gb_done = (sem(n) for n in (
            "sel_ready", "selt_full", "selt_done", "oh_ready", "gb_full", "gb_done"))
        u_in, v_in = [sem(f"u_in{i}") for i in range(2)], [sem(f"v_in{i}") for i in range(2)]
        hd_full, ge_done, yd_ready, vd_full = (sem(n) for n in ("hd_full", "ge_done", "yd_ready", "vd_full"))
        row_in = [sem(f"row_in{i}") for i in range(RING)]
        dve_seq, act_seq, lam_step, lam_act = sem("dve_seq"), sem("act_seq"), sem("lam_step"), sem("lam_act")

        tiles = ([(w_in, COL_XBC), (w_in, COL_XBC + HALF), (w_in, COL_Z), (w_in, COL_Q), (w_in, COL_K),
                  (w_in, COL_V), (w_out, 0), (w_out, HALF)] + [(w_q, i * HALF) for i in range(4)])
        products_of = ([(proj_full, k) for k in (5, 9, 13, 17, 22, 26)] + [(res_full, NB), (res_full, 2 * NB)]
                       + [(q2_full, 4 * (i + 1)) for i in range(4)])
        WDT = TMP[:, 0, 0:KC * NH]

        v_j = v.rearrange("(i j) n -> j i n", j=NKEY)

        ROUTES = [2, 3, 0, 1]
        PAIRS = NKEY // (2 * 2 * HB)

        STEPS = ["S1", "A0", "S2", "A1", "B0", "A2", "B1", "S3", "A3", "B2", "B3", "N"]

        block = ctx.enter_context(nc.Block())

        @block.sync
        def _(sp):
            for b in range(NB):
                sp.dma_start(X[:, b, :], x[b * P:(b + 1) * P, :]).then_inc(ld_x[b], 16)
                if b == 0:
                    sp.dma_start(CONST[:], consts).then_inc(ld_par, 16)
                    sp.dma_start(COLS[:], cols).then_inc(ld_par, 16)
                    sp.dma_start(ROWS[:], rows).then_inc(ld_par, 16)
                    sp.dma_start(WDT.rearrange("p (c n) -> p c n", n=NH),
                                 w_in[:, COL_DT:COL_DT + NH].rearrange("(c p) n -> p c n", p=P)).then_inc(ld_par, 16)
            n = 0
            for mat, c0 in tiles:
                if n == 16:
                    sp.wait_ge(y_ready, 2 * NB)
                    sp.dma_start(KEYS, keys_t).then_inc(ld_keys, 16)
                    sp.dma_start(FW, ffn_w).then_inc(ld_keys, 16)
                for half in range(2):
                    if n >= NHALFW and half == 0:
                        sp.wait_ge(*products_of[n // 2 - 2])
                    src = mat[half * 4 * P:(half + 1) * 4 * P, c0:c0 + HALF].rearrange("(c p) n -> p c n", p=P)
                    sp.dma_start(W[:, n % NHALFW, :].rearrange("p (c n) -> p c n", n=HALF), src)\
                        .then_inc(w_full[n % NHALFW], 16)
                    n += 1

            def load_tiles(it, first):
                for q in range(2):
                    if first:
                        sp.wait_ge(q2_full, 2 * PH)
                    else:
                        sp.wait_ge(hd_full, it * 2 + (q - 1))
                    sp.dma_start(UT[:, q], u_t[bass.ds(it * 2 + q, 1)].rearrange("j p (c i) -> p (j c) i", c=KC))\
                        .then_inc(u_in[q], 16)
                for q in range(2):
                    if first:
                        sp.wait_ge(gb_full, HT // NG_TOK)
                    else:
                        sp.wait_ge(vd_full, it * 2 + (q - 1))
                    sp.dma_start(VT[:, q, :], v_j[bass.ds(it * 2 + q, 1)].rearrange("j p n -> p (j n)"))\
                        .then_inc(v_in[q], 16)

            load_tiles(0, True)
            with sp.Fori(1, NKEY // 2, 1) as it:
                load_tiles(it, False)
            for b in range(NB):
                sp.wait_ge(out_ready, b + 1)
                sp.dma_start(out[b * P:(b + 1) * P, :], X[:, b, :]).then_inc(stored, 16)
            sp.wait_ge(stored, 16 * NB)

        @block.tensor
        def _(pe):
            tile = [0]

            def transpose_block(kind, b):
                pe.wait_ge(y_ready, kind * NB + b + 1)
                for c in range(2):
                    j = (kind * NB + b) * 2 + c
                    if j >= 4:
                        pe.wait_ge(t_done, j - 3)
                    if kind == 1 and j < 20:
                        pe.wait_ge(y_free, 4 * NB)
                        pe.wait_ge(o_free, NB)
                    for i in range(4):
                        last = nc.tensor.transpose(PS[j % 4][:, i * P:(i + 1) * P],
                                                   Y[:, b, (4 * c + i) * P:(4 * c + i + 1) * P], IDENT)
                    last.then_inc(t_full, 1)

            def weights_in():
                n = tile[0]
                tile[0] += 2
                for half in range(2):
                    pe.wait_ge(w_full[(n + half) % NHALFW], 16 * ((n + half) // NHALFW + 1))
                return n

            job = [0]

            def next_bank():
                j = job[0]
                job[0] += 1
                if j >= 4:
                    pe.wait_ge(proj_free, j - 3)
                return PS[4 + j % 4]

            pe.wait_ge(ld_par, 64)
            for b in range(NB):
                transpose_block(0, b)
            pe.wait_ge(t_done, 2 * NB)

            bank = next_bank()
            for b in range(NB):
                for c in range(KC):
                    last = nc.tensor.matmul(bank[:, b * NH:(b + 1) * NH], T8[:, b // 2, c, b % 2 * P:(b % 2 + 1) * P],
                                            WDT[:, c * NH:(c + 1) * NH], start=(c == 0), stop=(c == KC - 1))
            last.then_inc(proj_full, 1)
            for tl in range(2):
                n = weights_in()
                for cb in range(4):
                    bank = next_bank()
                    for c in range(KC):
                        wt = W[:, (n + c // 4) % NHALFW, (c % 4) * HALF + cb * P:(c % 4) * HALF + (cb + 1) * P]
                        last = nc.tensor.matmul(bank[:, :], wt, T8[:, :, c, :], start=(c == 0), stop=(c == KC - 1))
                    last.then_inc(proj_full, 1)
            for tl in range(4):
                n = weights_in()
                for b in range(NB):
                    bank = next_bank()
                    for c in range(KC):
                        wt = W[:, (n + c // 4) % NHALFW, (c % 4) * HALF:(c % 4 + 1) * HALF]
                        last = nc.tensor.matmul(bank[:, :], T8[:, b // 2, c, b % 2 * P:(b % 2 + 1) * P], wt,
                                                start=(c == 0), stop=(c == KC - 1))
                    last.then_inc(proj_full, 1)
                if tl == 1:
                    pe.wait_ge(da_ready, 1)
                    bank = next_bank()
                    for b in range(NB):
                        nc.tensor.matmul(bank[:, b * 16:b * 16 + NH], TRI, DA[:, b, :], start=True, stop=True)
                        last = nc.tensor.matmul(bank[:, b * 16 + NH:b * 16 + 16], ONES[:, :], DA[:, b, :],
                                                start=True, stop=True)
                    last.then_inc(proj_full, 1)
            for i, src in enumerate((Q, K)):
                for b in range(NB):
                    pe.wait_ge(qk_ready, i * NB + b + 1)
                    bank = next_bank()
                    for h in range(DH):
                        last = nc.tensor.transpose(bank[:, h * P:(h + 1) * P], src[:, b, h * P:(h + 1) * P], IDENT)
                    last.then_inc(proj_full, 1)

            pe.wait_ge(proj_free, job[0])
            pe.wait_ge(xc_done, CB)

            def scores(b, h):
                i = b * DH + h
                if i >= 2:
                    pe.wait_ge(exp_done, 2 * (i - 1))
                for j in range(2):
                    last = nc.tensor.matmul(PS[4 + 2 * (i % 2) + j][:, 0:P * (b + 1)],
                                            QT[j * QKD:(j + 1) * QKD, h, b * P:(b + 1) * P],
                                            KT[j * QKD:(j + 1) * QKD, h, 0:P * (b + 1)], start=True, stop=True)
                    last.then_inc(sc_full, 1)

            def values(b, h):
                i = b * DH + h
                pe.wait_ge(at_ready, i + 1)
                if i >= 1:
                    pe.wait_ge(att_done, i)
                for kb in range(b + 1):
                    last = nc.tensor.transpose(PS[3][:, kb * P:(kb + 1) * P],
                                               PP[:, i % 2, 0, kb * P:(kb + 1) * P], IDENT)
                last.then_inc(att_full, 1)
                pe.wait_ge(att_done, i + 1)
                if h == 0:
                    pe.wait_ge(y_free, 4 * b + 2)
                for kb in range(b + 1):
                    last = nc.tensor.matmul(PS[2][:, h * P:(h + 1) * P], AT[:, kb * P:(kb + 1) * P],
                                            V[:, kb, h * P:(h + 1) * P], start=(kb == 0), stop=(kb == b))
                last.then_inc(pv_full, 1)

            for b in range(NB):
                tok = slice(b * P, (b + 1) * P)
                for step in STEPS:
                    if step == "S1":
                        if b:
                            pe.wait_ge(y_free, 4 * b)
                            pe.wait_ge(o_free, b)
                        for i in range(4):
                            last = nc.tensor.transpose(PS[0][:, i * P:(i + 1) * P], XC[:, i, tok], IDENT)
                        last.then_inc(ssd_in, 1)
                        for g in range(NG):
                            nc.tensor.transpose(PS[1][:, g * P:(g + 1) * P], XC[:, 4 + g, tok], IDENT)
                        for g in range(NG):
                            last = nc.tensor.matmul(PS[1][:, (2 + g) * P:(3 + g) * P], XC[:, 4 + g, tok],
                                                    XC[:, 6 + g, tok], start=True, stop=True)
                        last.then_inc(ssd_in, 1)
                        pe.wait_ge(dab_ready, b + 1)
                        for g in range(NG):
                            if g:
                                pe.wait_ge(seg_ready, b * NG + g)
                            for h in range(HPG):
                                last = nc.tensor.matmul(PS[2][:, h * P:(h + 1) * P], DAB[:, g * HPG + h, :], TRI,
                                                        start=True, stop=True)
                            last.then_inc(seg_full, 1)
                    elif step == "S2":
                        pe.wait_ge(m_ready, b * NG + NG)
                        pe.wait_ge(xdt_ready, 2 * b + 1)
                        pe.wait_ge(ssd_in_free, 3 * b + 1)
                        for h in range(NH):
                            last = nc.tensor.matmul(PS[0][:, h * HD:(h + 1) * HD],
                                                    SEG[:, h // HPG, (h % HPG) * P:(h % HPG + 1) * P],
                                                    XDT[:, h * HD:(h + 1) * HD], start=True, stop=True)
                        last.then_inc(y_full, 1)
                        pe.wait_ge(seg_ready, b * NG + NG)
                        if b:
                            pe.wait_ge(st_ready, b)
                            for g in range(NG):
                                last = nc.tensor.matmul(PS[2][:, g * 256:(g + 1) * 256], XC[:, 6 + g, tok],
                                                        ST[:, g * 256:(g + 1) * 256], start=True, stop=True)
                            last.then_inc(yoff_full, 1)
                        pe.wait_ge(ssd_in_free, 3 * b + 3)
                        pe.wait_ge(xdt_ready, 2 * b + 2)
                        for g in range(NG):
                            last = nc.tensor.matmul(PS[1][:, g * 256:(g + 1) * 256], BM[:, g * P:(g + 1) * P],
                                                    XDTE[:, g * 256:(g + 1) * 256], start=True, stop=True)
                        last.then_inc(st_full, 1)
                    elif step[0] == "A":
                        scores(b, int(step[1]))
                    elif step[0] == "B":
                        values(b, int(step[1]))

            for b in range(NB):
                transpose_block(1, b)
            pe.wait_ge(t_done, 4 * NB)
            rj = 0
            for tl in range(2):
                n = weights_in()
                for b in range(NB):
                    if rj >= 4:
                        pe.wait_ge(res_free, rj - 3)
                    else:
                        pe.wait_ge(exp_done, 2 * DH * NB)
                    for c in range(KC):
                        wt = W[:, (n + c // 4) % NHALFW, (c % 4) * HALF:(c % 4 + 1) * HALF]
                        last = nc.tensor.matmul(PS[4 + rj % 4][:, :], T8[:, b // 2, c, b % 2 * P:(b % 2 + 1) * P], wt,
                                                start=(c == 0), stop=(c == KC - 1))
                    last.then_inc(res_full, 1)
                    rj += 1
            for b in range(NB):
                transpose_block(2, b)
            pe.wait_ge(t_done, 6 * NB)
            for j in range(2 * PH):
                if j % 4 == 0:
                    n = weights_in()
                if j < 4:
                    pe.wait_ge(res_free, 2 * NB)
                else:
                    pe.wait_ge(q2_done, j - 3)
                for c in range(KC):
                    wt = W[:, (n + c // 4) % NHALFW, (c % 4) * HALF + (j % 4) * P:(c % 4) * HALF + (j % 4 + 1) * P]
                    last = nc.tensor.matmul(PS[4 + j % 4][:, :], wt, T8[:, :, c, :], start=(c == 0), stop=(c == KC - 1))
                last.then_inc(q2_full, 1)
            pe.wait_ge(q2_done, 2 * PH)
            pe.wait_ge(ld_keys, 32)
            for b in range(NB):
                for c in range(4):
                    j = b * 4 + c
                    if j >= 4:
                        pe.wait_ge(ks_done, j - 3)
                    for i in range(4):
                        hj = 4 * c + i
                        last = nc.tensor.matmul(PS[j % 4][:, i * P:(i + 1) * P],
                                                Q2[hj // 8][:, hj % 8, b * P:(b + 1) * P], KEYS[:, hj, :],
                                                start=True, stop=True)
                    last.then_inc(ks_full, 1)

            for n, b in enumerate(range(HB, NB)):
                pe.wait_ge(sel_ready, n + 1)
                pe.wait_ge(ks_done, 4 * NB)
                for a, src in enumerate((ISELS[:, b, 0, :], ISELS[:, b, 1, :], G[:, b, :])):
                    last = nc.tensor.transpose(PS[4 + n][:, a * P:(a + 1) * P], src, IDENT)
                last.then_inc(selt_full, 1)

            def weights_of_tokens(it, first):
                for q in range(2):
                    pe.wait_ge(oh_ready, it * 2 + (q + 1))
                    if not first:
                        pe.wait_ge(gb_done, it * 2 + (q - 1))
                    for i in range(NG_TOK):
                        last = nc.tensor.matmul(PS[2 + q][:, i * P:(i + 1) * P], ONEHOT[:, q, i, 0, :],
                                                ONEHOT[:, q, i, 1, :], start=True, stop=True)
                    last.then_inc(gb_full, 1)

            weights_of_tokens(0, True)
            with pe.Fori(1, HT // NG_TOK // 2, 1) as it:
                weights_of_tokens(it, False)

            def hidden(q, it, first):
                pe.wait_ge(u_in[q], it * 16 + 16)
                if not first:
                    pe.wait_ge(ge_done, it * 2 + (q - 1))
                for c in range(KC):
                    last = nc.tensor.matmul(PS[q][:, 0:HT], UT[:, q, c, :], T8[:, 1, c, :],
                                            start=(c == 0), stop=(c == KC - 1))
                last.then_inc(hd_full, 1)

            def products(q, it, first=False, final=False):
                pe.wait_ge(v_in[q], it * 16 + 16)
                pe.wait_ge(yd_ready, it * 2 + (q + 1))
                for t in range(HB):
                    for n in range(2):
                        last = nc.tensor.matmul(PS[4 + 2 * t + n][:, :], GE[:, q, t * P:(t + 1) * P],
                                                VT[:, q, n * HALF:(n + 1) * HALF], start=first, stop=final,
                                                skip_group_check=True)
                last.then_inc(vd_full, 1)

            hidden(0, 0, True)
            hidden(1, 0, True)
            pe.wait_ge(selt_done, HB)
            products(0, 0, first=True)
            with pe.Fori(1, NKEY // 2, 1) as it:
                hidden(0, it, False)
                products(1, it - 1)
                hidden(1, it, False)
                products(0, it)
            products(1, NKEY // 2 - 1, final=True)

        @block.scalar
        def _(act):
            seq = [0]

            def sums_of_squares(kind):
                for b in range(NB):
                    if kind == 0:
                        act.wait_ge(ld_x[b], 16)
                    else:
                        act.wait_ge(res_free, NB + b + 1)
                    if kind == 1 and b == 0:
                        act.wait_ge(t_full, 4 * NB)
                    nc.scalar.activation(Y[:, b, :], X[:, b, :], ACT.Square,
                                         accum_out=SS[:, b:b + 1]).then_inc(sq_done, 1)
                act.wait_ge(rs_half, kind + 1)
                nc.scalar.activation(SS[:, 0:NB], SS[:, 0:NB], ACT.Sqrt).then_inc(rs_done, 1)

            sums_of_squares(0)
            job = [0]

            def drain_bank(dst, func=ACT.Copy, view=None):
                j = job[0]
                job[0] += 1
                act.wait_ge(proj_full, j + 1)
                src = PS[4 + j % 4][:, :] if view is None else view(PS[4 + j % 4])
                nc.scalar.activation(dst, src, func).then_inc(proj_free, 1)

            drain_bank(DT[:, :, :].rearrange("p b h -> p (b h)"), view=lambda t: t[:, 0:NB * NH])
            act.wait_ge(dt_step, 1)
            nc.scalar.activation(DTS[:, 1], DTS[:, 0], ACT.Exp, scale=-1.0).then_inc(dt_act, 1)
            act.wait_ge(dt_step, 2)
            nc.scalar.activation(DTS[:, 3], DTS[:, 2], ACT.Ln).then_inc(dt_act, 1)
            nc.scalar.activation(AH[:, :], ROWS[:, R_ALOG:R_ALOG + NH], ACT.Exp).then_inc(dt_act, 1)
            act.wait_ge(lam_step, 2)
            nc.scalar.activation(LAM[:, 2:4], LAM[:, 0:2], ACT.Exp).then_inc(lam_act, 1)
            for cb in range(CB):
                drain_bank(XBC[:, cb, CONVW - 1:])
            for b in range(NB):
                drain_bank(Z[:, b, :], ACT.Silu)
            for cb in range(CB):
                act.wait_ge(conv_done, cb + 1)
                nc.scalar.activation(XC[:, cb, :], XC[:, cb, :], ACT.Silu,
                                     bias=COLS[:, V_CB + cb:V_CB + cb + 1]).then_inc(xc_done, 1)
            for b in range(NB):
                drain_bank(Q[:, b, :])
            drain_bank(ACS[:, :, :].rearrange("p b h -> p (b h)"), view=lambda t: t[:, 0:NB * 2 * NH])
            for dst in (K, V):
                for b in range(NB):
                    drain_bank(dst[:, b, :])
            act.wait_ge(proj_free, 18)
            nc.scalar.activation(EACS[:, :, :], ACS[:, :, 0:NH], ACT.Exp).then_inc(dt_act, 1)
            nc.scalar.activation(CD[:, :, :], ACS[:, :, NH:2 * NH], ACT.Exp).then_inc(dt_act, 1)
            act.wait_ge(dt_step, 3)
            nc.scalar.activation(DTE[:, :, :], DTE[:, :, :], ACT.Exp).then_inc(dt_act, 1)
            for i in range(2):
                act.wait_ge(yrs_half, i + 1)
                nc.scalar.activation(SS[:, 0:8 * NB], SS[:, 0:8 * NB], ACT.Sqrt).then_inc(yrs_done, 1)
            for dst in (QT, KT):
                for b in range(NB):
                    drain_bank(dst[:, :, b * P:(b + 1) * P], view=lambda t: t[:, :].rearrange("p (h n) -> p h n", n=P))

            def exps(b, h):
                i = b * DH + h
                act.wait_ge(mx_ready, i + 1)
                if i >= 2:
                    act.wait_ge(att_full, i - 1)
                for j in range(2):
                    nc.scalar.activation(PP[:, i % 2, j, 0:P * (b + 1)], PS[4 + 2 * (i % 2) + j][:, 0:P * (b + 1)],
                                         ACT.Exp, bias=NMX[:, i % 2, j:j + 1], scale=QKD ** -0.5,
                                         accum_out=SUMS[:, i % 2, j:j + 1]).then_inc(exp_done, 1)

            for b in range(NB):
                for step in STEPS:
                    if step == "S1":
                        if b:
                            act.wait_ge(y_free, 4 * b)
                            act.wait_ge(st_full, b)
                        act.wait_ge(ssd_in, 2 * b + 1)
                        nc.scalar.activation(XS[:, :], PS[0][:, :], ACT.Copy).then_inc(ssd_in_free, 1)
                        act.wait_ge(ssd_in, 2 * b + 2)
                        nc.scalar.activation(BM[:, :], PS[1][:, 0:NG * P], ACT.Copy).then_inc(ssd_in_free, 1)
                        for g in range(NG):
                            act.wait_ge(seg_ready, b * NG + g + 1)
                            nc.scalar.activation(SEG[:, g, :], SEG[:, g, :], ACT.Exp).then_inc(seg_exp, 1)
                    elif step[0] == "A":
                        exps(b, int(step[1]))
                    elif step[0] == "B":
                        i = b * DH + int(step[1])
                        act.wait_ge(att_full, i + 1)
                        if i:
                            act.wait_ge(pv_full, i)
                        nc.scalar.activation(AT[:, 0:P * (b + 1)], PS[3][:, 0:P * (b + 1)], ACT.Copy)\
                            .then_inc(att_done, 1)
                    elif step == "N":
                        act.wait_ge(yrs_half, 2 + b + 1)
                        nc.scalar.activation(SMALL[:, 0:6], SMALL[:, 0:6], ACT.Sqrt).then_inc(yrs_done, 1)

            sums_of_squares(1)
            for j in range(2 * PH):
                act.wait_ge(q2_full, j + 1)
                nc.scalar.activation(Q2[j // 8][:, j % 8, :], PS[4 + j % 4][:, :], ACT.Copy).then_inc(q2_done, 1)
            for j in range(4 * NB):
                act.wait_ge(ks_full, j + 1)
                nc.scalar.activation(SC[:, j // 4, j % 4, :], PS[j % 4][:, :], ACT.Copy).then_inc(ks_done, 1)
            for n, b in enumerate(ROUTES):
                act.wait_ge(g_raw, n + 1)
                nc.scalar.activation(G[:, b, :], G[:, b, :], ACT.Exp).then_inc(g_exp, 1)
                if b >= HB:
                    act.wait_ge(selt_full, b - HB + 1)
                    nc.scalar.activation(KT3[:, :, (b - HB) * P:(b - HB + 1) * P],
                                         PS[4 + b - HB][:, 0:3 * P].rearrange("p (a n) -> p a n", a=3), ACT.Copy)\
                        .then_inc(selt_done, 1)
            with act.Fori(0, HT // NG_TOK // 2, 1) as it:
                for q in range(2):
                    act.wait_ge(gb_full, it * 2 + (q + 1))
                    nc.scalar.activation(GD[:, bass.ds((it * 2 + q) * NG_TOK, NG_TOK), :],
                                         PS[2 + q][:, :].rearrange("p (t j) -> p t j", j=NKEY), ACT.Copy)\
                        .then_inc(gb_done, 1)

            def gelus(it, first):
                for q in range(2):
                    act.wait_ge(hd_full, it * 2 + (q + 1))
                    if not first:
                        act.wait_ge(vd_full, it * 2 + (q - 1))
                    nc.scalar.activation(GE[:, q, :], PS[q][:, 0:HT], ACT.Gelu).then_inc(ge_done, 1)

            for seg in range(2 * HB):
                if seg == 0:
                    gelus(0, True)
                with act.Fori(PAIRS * seg + (seg == 0), PAIRS * (seg + 1), 1) as it:
                    gelus(it, False)
                if seg % 2 == 0:
                    act.wait_ge(h_ready, seg // 2 + 1)
                    nc.scalar.activation(H[:, :], H[:, :], ACT.Gelu).then_inc(gelu_done, 1)

        @block.vector
        def _(dve):
            seq = [0]

            def link(ins):
                seq[0] += 1
                ins.then_inc(dve_seq, 1)
                dve.wait_ge(dve_seq, seq[0])

            tt, ts, stt = nc.vector.tensor_tensor, nc.vector.tensor_scalar, nc.vector.scalar_tensor_tensor

            def inverse_mean(dst, src, n):
                link(ts(dst, src, 1.0 / n, EPS, ALU.mult, ALU.add))
                return nc.vector.reciprocal(dst, dst)

            def evacuate_transposes(kind):
                for b in range(NB):
                    for c in range(2):
                        j = (kind * NB + b) * 2 + c
                        dve.wait_ge(t_full, j + 1)
                        src = PS[j % 4][:, :].rearrange("p (i n) -> p i n", n=P)
                        dst = T8[:, b // 2, 4 * c:4 * c + 4, b % 2 * P:(b % 2 + 1) * P]
                        if kind == 0:
                            w = COLS[:, V_MIX + 4 * c:V_MIX + 4 * c + 4]
                            tt(dst, src, bc(w, 2, P), ALU.mult).then_inc(t_done, 1)
                        elif kind == 1:
                            tt(dst, src, bc(WC[:, 4 * c:4 * c + 4], 2, P), ALU.mult).then_inc(t_done, 1)
                        else:
                            nc.vector.tensor_copy(dst, src).then_inc(t_done, 1)

            nc.vector.memset(ONES[:, :], 1.0)
            nc.vector.memset(XBC[:, :, 0:CONVW - 1], 0.0)
            link(nc.vector.memset(ST[:, :], 0.0))
            dve.wait_ge(ld_par, 64)
            nc.vector.tensor_copy(WC[:, 0:4], COLS[:, V_SSD:V_SSD + 4])
            link(ts(WC[:, 4:8], COLS[:, V_SUB:V_SUB + 1].broadcast_to([P, 4]), 1.0 - LAMBDA_INIT, None, ALU.mult))
            dve.wait_ge(sq_done, NB)
            inverse_mean(SS[:, 0:NB], SS[:, 0:NB], DM).then_inc(rs_half, 1)
            dve.wait_ge(rs_done, 1)
            for b in range(NB):
                ts(Y[:, b, :], X[:, b, :], SS[:, b:b + 1], None, ALU.mult).then_inc(y_ready, 1)
            evacuate_transposes(0)

            dt = DT[:, :, :].rearrange("p b h -> p (b h)")
            dve.wait_ge(proj_free, 1)
            link(tt(DT[:, :, :], DT[:, :, :], bc(ROWS[:, R_DTB:R_DTB + NH], 1, NB), ALU.add))
            stt(DTS[:, 0], dt, -1.0, dt, ALU.mult, ALU.max).then_inc(dt_step, 1)
            dve.wait_ge(dt_act, 1)
            ts(DTS[:, 2], DTS[:, 1], 1.0, None, ALU.add).then_inc(dt_step, 1)
            dve.wait_ge(dt_act, 2)
            link(ts(DTS[:, 4], DTS[:, 2], 1.0, None, ALU.is_equal))
            link(tt(DTS[:, 3], DTS[:, 3], DTS[:, 4], ALU.add))
            link(stt(DTS[:, 5], DTS[:, 2], -1.0, DTS[:, 4], ALU.add, ALU.add))
            link(nc.vector.reciprocal(DTS[:, 5], DTS[:, 5]))
            link(tt(DTS[:, 3], DTS[:, 3], DTS[:, 5], ALU.mult))
            link(tt(DTS[:, 3], DTS[:, 3], DTS[:, 1], ALU.mult))
            link(stt(dt, dt, 0.0, DTS[:, 3], ALU.max, ALU.add))
            dve.wait_ge(dt_act, 3)
            stt(DA[:, :, :], DT[:, :, :], -1.0, bc(AH[:, :], 1, NB), ALU.mult, ALU.mult).then_inc(da_ready, 1)
            for i in range(2):
                a = ROWS[:, R_L + 128 * i:R_L + 128 * i + QKD]
                c = ROWS[:, R_L + 128 * i + QKD:R_L + 128 * i + 128]
                link(stt(LT[:, :], a, 1.0, c, ALU.mult, ALU.mult))
                nc.vector.reduce_sum(LAM[:, i:i + 1], LT[:, :], AXX).then_inc(lam_step, 1)
                dve.wait_ge(lam_step, i + 1)
            dve.wait_ge(lam_act, 1)
            link(tt(LAM[:, 4:5], LAM[:, 2:3], LAM[:, 3:4], ALU.subtract))
            link(ts(LAM[:, 4:5], LAM[:, 4:5], LAMBDA_INIT, -1.0, ALU.add, ALU.mult))

            for cb in range(CB):
                dve.wait_ge(proj_free, 2 + cb)
                w = lambda k: COLS[:, V_CW + cb * CONVW + k:V_CW + cb * CONVW + k + 1]
                link(ts(XC[:, cb, :], XBC[:, cb, 0:SEQ], w(0), None, ALU.mult))
                for k in range(1, CONVW):
                    ins = stt(XC[:, cb, :], XBC[:, cb, k:k + SEQ], w(k), XC[:, cb, :], ALU.mult, ALU.add)
                    if k < CONVW - 1:
                        link(ins)
                ins.then_inc(conv_done, 1)

            for i, (src, first) in enumerate(((Q, 14), (K, 19))):
                nw = ROWS[:, (R_QN, R_KN)[i]:(R_QN, R_KN)[i] + QKD]
                for b in range(NB):
                    dve.wait_ge(proj_free, first + b)
                    link(tt(TMP[:, 0, :], src[:, b, :], src[:, b, :], ALU.mult))
                    link(nc.vector.reduce_sum(SS[:, 8 * b:8 * b + 8],
                                              TMP[:, 0, :].rearrange("p (g d) -> p g d", d=QKD), AXX))
                inverse_mean(SS[:, 0:8 * NB], SS[:, 0:8 * NB], QKD).then_inc(yrs_half, 1)
                if i == 0:
                    dve.wait_ge(proj_free, 18)
                    tt(DTE[:, :, :], ACS[:, :, NH:2 * NH], ACS[:, :, 0:NH], ALU.subtract).then_inc(dt_step, 1)
                dve.wait_ge(yrs_done, i + 1)
                for b in range(NB):
                    h3 = src[:, b, :].rearrange("p (g d) -> p g d", d=QKD)
                    link(tt(h3, h3, bc(SS[:, 8 * b:8 * b + 8], 2, QKD), ALU.mult))
                    link(tt(h3, h3, bc(nw, 1, 8), ALU.mult))
                    cos = bc(CONST[:, C_COS + b * RD:C_COS + (b + 1) * RD], 1, 8)
                    sin = bc(CONST[:, C_SIN + b * RD:C_SIN + (b + 1) * RD], 1, 8)
                    t = [TMP[:, 1, 64 * k:64 * k + 64].rearrange("p (g d) -> p g d", d=RD) for k in range(4)]
                    tt(t[0], h3[:, :, 0:RD], cos, ALU.mult)
                    tt(t[1], h3[:, :, RD:2 * RD], sin, ALU.mult)
                    tt(t[2], h3[:, :, 0:RD], sin, ALU.mult)
                    link(tt(t[3], h3[:, :, RD:2 * RD], cos, ALU.mult))
                    tt(h3[:, :, 0:RD], t[0], t[1], ALU.subtract)
                    tt(h3[:, :, RD:2 * RD], t[2], t[3], ALU.add).then_inc(qk_ready, 1)
                    dve.wait_ge(qk_ready, i * NB + b + 1)

            hd3 = lambda ap: ap.rearrange("p (h d) -> p h d", d=HD)
            for b in range(NB):
                i0 = b * DH
                for step in STEPS:
                    if step == "S1":
                        if b:
                            dve.wait_ge(seg_full, NG * b)
                            dve.wait_ge(st_full, b)
                        nc.vector.tensor_copy(DAB[:, :, :], bc(DA[:, b, :], 2, P)).then_inc(dab_ready, 1)
                        for g in range(NG):
                            dve.wait_ge(seg_full, NG * b + g + 1)
                            for h in range(HPG):
                                hh = g * HPG + h
                                last = ts(SEG[:, g, h * P:(h + 1) * P], PS[2][:, h * P:(h + 1) * P],
                                          ACS[:, b, hh:hh + 1], 0.0, ALU.subtract, ALU.min)
                            last.then_inc(seg_ready, 1)
                        dve.wait_ge(ssd_in_free, 3 * b + 2)
                        tt(CBM[:, :, :], PS[1][:, NG * P:2 * NG * P].rearrange("p (g n) -> p g n", n=P),
                           bc(TRI, 1, NG), ALU.mult).then_inc(ssd_in_free, 1)
                        dve.wait_ge(ssd_in_free, 3 * b + 3)
                        tt(hd3(XDT[:, :]), hd3(XS[:, :]), bc(DT[:, b, :], 2, HD), ALU.mult).then_inc(xdt_ready, 1)
                        dve.wait_ge(xdt_ready, 2 * b + 1)
                        dve.wait_ge(dt_act, 6)
                        tt(hd3(XDTE[:, :]), hd3(XDT[:, :]), bc(DTE[:, b, :], 2, HD), ALU.mult).then_inc(xdt_ready, 1)
                        for g in range(NG):
                            dve.wait_ge(seg_exp, NG * b + g + 1)
                            m = SEG[:, g, :].rearrange("p (h n) -> p h n", n=P)
                            tt(m, m, bc(CBM[:, g, :], 1, HPG), ALU.mult).then_inc(m_ready, 1)
                    elif step == "S2":
                        y = Y[:, b, 0:SSDW]
                        link(tt(hd3(y), hd3(XS[:, :]), bc(ROWS[:, R_D:R_D + NH], 2, HD), ALU.mult))
                        dve.wait_ge(y_full, b + 1)
                        tt(y, y, PS[0][:, :], ALU.add).then_inc(y_free, 1)
                        dve.wait_ge(y_free, 4 * b + 1)
                        if b:
                            dve.wait_ge(yoff_full, b)
                            link(tt(hd3(TMP[:, 0, :]), hd3(PS[2][:, :]), bc(EACS[:, b, :], 2, HD), ALU.mult))
                            tt(y, y, TMP[:, 0, :], ALU.add).then_inc(y_free, 1)
                        else:
                            nc.vector.tensor_copy(TMP[:, 0, 0:2], TMP[:, 0, 2:4]).then_inc(y_free, 1)
                        dve.wait_ge(y_free, 4 * b + 2)
                    elif step == "S3":
                        dve.wait_ge(st_full, b + 1)
                        link(tt(hd3(ST[:, :]), hd3(ST[:, :]), bc(CD[:, b, :], 2, HD), ALU.mult))
                        tt(ST[:, :], ST[:, :], PS[1][:, :], ALU.add).then_inc(st_ready, 1)
                        dve.wait_ge(st_ready, b + 1)
                        y = Y[:, b, 0:SSDW]
                        link(tt(y, y, Z[:, b, :], ALU.mult))
                        tt(TMP[:, 0, :], y, y, ALU.mult).then_inc(y_free, 1)
                        dve.wait_ge(y_free, 4 * b + 3)
                        nc.vector.reduce_sum(SMALL[:, 0:NG], TMP[:, 0, :].rearrange("p (g d) -> p g d", g=NG), AXX)\
                            .then_inc(y_free, 1)
                        dve.wait_ge(y_free, 4 * b + 4)
                    elif step[0] == "A":
                        i = i0 + int(step[1])
                        for j in range(2):
                            bank = PS[4 + 2 * (i % 2) + j]
                            dve.wait_ge(sc_full, 2 * i + j + 1)
                            link(nc.vector.memset(bank[0:64, b * P + 64:(b + 1) * P], NEG))
                            link(nc.vector.reduce_max(MX[:, i % 2, j:j + 1], bank[:, 0:P * (b + 1)], AXX))
                        if i >= 2:
                            dve.wait_ge(exp_done, 2 * (i - 1))
                        ts(NMX[:, i % 2, :], MX[:, i % 2, :], -(QKD ** -0.5), None, ALU.mult).then_inc(mx_ready, 1)
                        dve.wait_ge(mx_ready, i + 1)
                    elif step[0] == "B":
                        i = i0 + int(step[1])
                        n = P * (b + 1)
                        dve.wait_ge(exp_done, 2 * i + 2)
                        link(nc.vector.reciprocal(RS[:, i % 2, :], SUMS[:, i % 2, :]))
                        link(ts(RS[:, i % 2, 1:2], RS[:, i % 2, 1:2], LAM[:, 4:5], None, ALU.mult))
                        link(ts(PP[:, i % 2, 1, 0:n], PP[:, i % 2, 1, 0:n], RS[:, i % 2, 1:2], None, ALU.mult))
                        stt(PP[:, i % 2, 0, 0:n], PP[:, i % 2, 0, 0:n], RS[:, i % 2, 0:1], PP[:, i % 2, 1, 0:n],
                            ALU.mult, ALU.add).then_inc(at_ready, 1)
                        dve.wait_ge(at_ready, i + 1)
                    elif step == "N":
                        dve.wait_ge(pv_full, DH * (b + 1))
                        yd = Y[:, b, SSDW:DM]
                        nc.vector.tensor_copy(yd, PS[2][:, :]).then_inc(o_free, 1)
                        dve.wait_ge(o_free, b + 1)
                        link(tt(TMP[:, 1, :], yd, yd, ALU.mult))
                        link(nc.vector.reduce_sum(SMALL[:, 2:6], TMP[:, 1, :].rearrange("p (g d) -> p g d", d=VD), AXX))
                        ts(SMALL[:, 0:2], SMALL[:, 0:2], 1.0 / 256, EPS, ALU.mult, ALU.add)
                        link(ts(SMALL[:, 2:6], SMALL[:, 2:6], 1.0 / VD, EPS, ALU.mult, ALU.add))
                        nc.vector.reciprocal(SMALL[:, 0:6], SMALL[:, 0:6]).then_inc(yrs_half, 1)
                        dve.wait_ge(yrs_done, 2 + b + 1)
                        y3 = Y[:, b, 0:SSDW].rearrange("p (g d) -> p g d", g=NG)
                        tt(y3, y3, bc(SMALL[:, 0:2], 2, 256), ALU.mult)
                        y3 = yd.rearrange("p (g d) -> p g d", d=VD)
                        tt(y3, y3, bc(SMALL[:, 2:6], 2, VD), ALU.mult).then_inc(y_ready, 1)
                        dve.wait_ge(y_ready, NB + b + 1)

            evacuate_transposes(1)
            rj = 0
            for tl in range(2):
                for b in range(NB):
                    dve.wait_ge(res_full, rj + 1)
                    xb = X[:, b, tl * HALF:(tl + 1) * HALF]
                    tt(xb, xb, PS[4 + rj % 4][:, :], ALU.add).then_inc(res_free, 1)
                    rj += 1
            dve.wait_ge(sq_done, 2 * NB)
            inverse_mean(SS[:, 0:NB], SS[:, 0:NB], DM).then_inc(rs_half, 1)
            dve.wait_ge(rs_done, 2)
            dve.wait_ge(ld_keys, 32)
            for b in range(NB):
                stt(Y[:, b, :], X[:, b, :], SS[:, b:b + 1], FW[:, :], ALU.mult, ALU.mult).then_inc(y_ready, 1)
            evacuate_transposes(2)

            def top16(vals, values, places):
                link(nc.vector.max(values[:, 0:8], vals))
                nc.vector.max_index(places[:, 0:8], values[:, 0:8], vals)
                link(nc.vector.match_replace(vals, values[:, 0:8], vals, NEG))
                link(nc.vector.max(values[:, 8:16], vals))
                link(nc.vector.max_index(places[:, 8:16], values[:, 8:16], vals))

            def route(n, b):
                dve.wait_ge(ks_done, 4 * b + 4)
                sc = SC[:, b, :, :].rearrange("p a (i n) -> p (a i) n", n=NKEY)
                for h in range(PH):
                    for j in range(2):
                        top16(sc[:, 2 * h + j, :], TOPV[:, j, :], TOPI[:, h, j, :])
                    link(tt(CAND.rearrange("p (a c) -> p a c", c=TOPK), bc(TOPV[:, 0, :], 2, TOPK),
                            bc(TOPV[:, 1, :], 1, TOPK), ALU.add))
                    top16(CAND, TOPS[:, h, :], POS[:, h, :])
                tt(G[:, b, :].rearrange("p (h k) -> p h k", k=TOPK), TOPS[:, :, :],
                   TOPS[:, :, 0:1].broadcast_to([P, PH, TOPK]), ALU.subtract).then_inc(g_raw, 1)
                pos = POS[:, :, :].rearrange("p h k -> p (h k)")
                ts(PAB[:, 0, :], pos, 4, None, ALU.logical_shift_right)
                link(ts(PAB[:, 1, :], pos, 15, None, ALU.bitwise_and))
                nc.vector.tensor_copy(PABF[:, :, :], PAB[:, :, :])
                link(nc.vector.tensor_copy(TOPIF[:, :, :, :], TOPI[:, :, :, :]))
                for j in range(2):
                    for q in range(4):
                        oh = OH[:, q, :].rearrange("p (k c) -> p k c", c=TOPK)
                        ph = PABF[:, j, 32 * q:32 * q + 32]
                        link(tt(oh, bc(CONST[:, C_IOTA:C_IOTA + TOPK], 1, 32), bc(ph, 2, TOPK), ALU.is_equal))
                        for h2 in range(2):
                            o = OH[:, q, h2 * 256:(h2 + 1) * 256].rearrange("p (k c) -> p k c", c=TOPK)
                            link(tt(o, o, bc(TOPIF[:, 2 * q + h2, j, :], 1, TOPK), ALU.mult))
                        link(nc.vector.reduce_sum(ISELS[:, b, j, 32 * q:32 * q + 32], oh, AXX))
                if b < HB:
                    stt(IDX[:, b, :], ISELS[:, b, 0, :], float(NKEY), ISELS[:, b, 1, :], ALU.mult, ALU.add)\
                        .then_inc(idx_ready, 1)
                dve.wait_ge(g_exp, n + 1)
                g3 = G[:, b, :].rearrange("p (h k) -> p h k", k=TOPK)
                link(nc.vector.reduce_sum(SMALL[:, 8:16], g3, AXX))
                link(nc.vector.reciprocal(SMALL[:, 8:16], SMALL[:, 8:16]))
                last = tt(g3, g3, bc(SMALL[:, 8:16], 2, TOPK), ALU.mult)
                if b >= HB:
                    last.then_inc(sel_ready, 1)
                else:
                    link(last)

            for n, b in enumerate(ROUTES):
                route(n, b)

            iota = CONST[:, C_IOTA:C_IOTA + NKEY]

            def onehots(it, first):
                for q in range(2):
                    if not first:
                        dve.wait_ge(gb_full, it * 2 + (q - 1))
                    for i in range(NG_TOK):
                        t = (it * 2 + q) * NG_TOK + i
                        ts(ONEHOT[:, q, i, 0, :], iota, KT3[:, 0, bass.ds(t, 1)], None, ALU.is_equal)
                        last = ts(ONEHOT[:, q, i, 1, :], iota, KT3[:, 1, bass.ds(t, 1)],
                                  KT3[:, 2, bass.ds(t, 1)], ALU.is_equal, ALU.mult)
                    last.then_inc(oh_ready, 1)

            dve.wait_ge(selt_done, HB)
            onehots(0, True)
            with dve.Fori(1, HT // NG_TOK // 2, 1) as it:
                onehots(it, False)
            dve.wait_ge(gb_done, HT // NG_TOK)

            for seg in range(2 * HB):
                b, j0, slot0 = seg // 2, 2 * PAIRS * seg, NSLOT * seg
                with dve.Fori(0, PAIRS, 1) as it:
                    for q in range(2):
                        dve.wait_ge(ge_done, it * 2 + (j0 + q + 1))
                        tt(GE[:, q, :], GE[:, q, :], GD[:, :, bass.ds(it * 2 + (j0 + q), 1)].rearrange("p t j -> p (t j)"),
                           ALU.mult).then_inc(yd_ready, 1)
                        for r in range(q * STEP // 2, (q + 1) * STEP // 2):
                            dve.wait_ge(row_in[r % RING], it * (16 * STEP // RING) + 16 * ((slot0 + r) // RING + 1))
                            if seg % 2 == 0:
                                stt(UV[:, r % RING, :], UV[:, r % RING, :], 1.0, Y[:, b, :], ALU.mult, ALU.mult,
                                    accum_out=H[:, bass.ds(it * STEP + r, 1)]).then_inc(used, 1)
                            else:
                                dve.wait_ge(used, it * STEP + (slot0 + r))
                                stt(X[:, b, :], UV[:, r % RING, :], GH[:, bass.ds(it * STEP + r, 1)], X[:, b, :],
                                    ALU.mult, ALU.add).then_inc(used, 1)
                dve.wait_ge(used, slot0 + NSLOT)
                if seg % 2 == 0:
                    nc.vector.tensor_copy(GH[:, :], H[:, :]).then_inc(h_ready, 1)
                    dve.wait_ge(gelu_done, b + 1)
                    link(tt(GH[:, :], G[:, b, :], H[:, :], ALU.mult))
                else:
                    nc.vector.tensor_copy(SMALL[:, 0:2], SMALL[:, 2:4]).then_inc(out_ready, 1)
            dve.wait_ge(vd_full, NKEY)
            for t in range(HB):
                for n in range(2):
                    xb = X[:, HB + t, n * HALF:(n + 1) * HALF]
                    last = tt(xb, xb, PS[4 + 2 * t + n][:, :], ALU.add)
                last.then_inc(out_ready, 1)

        @block.gpsimd
        def _(pool):
            pool.wait_ge(q2_full, 2 * PH)

            def fetch(b, table, group, it, first):
                for half in range(2):
                    nc.gpsimd.tensor_copy(IXC[:, half, :], IDX[:, b, bass.ds(it * (2 * STEP) + half * STEP, STEP)])\
                        .then_inc(ixc_ready, 1)
                    pool.wait_ge(ixc_ready, it * 2 + (group + half + 1))
                    for r in range(STEP):
                        if not first or half or r >= RING:
                            pool.wait_ge(used, use)
                            pool.reg_add(use, use, 1)
                        pool.indirect_dma_start(UV[:, r % RING, :], None, table,
                                                bass.IndirectOffsetOnAxis(IXC[:, half, r:r + 1], 0))\
                            .then_inc(row_in[r % RING], 16)

            use = pool.alloc_register("use")
            pool.reg_mov(use, 1)
            group = 0
            for b in range(HB):
                pool.wait_ge(idx_ready, b + 1)
                for table in (u, v):
                    start = 1 if group == 0 else 0
                    if start:
                        fetch(b, table, group, 0, True)
                    with pool.Fori(start, NSLOT // (2 * STEP), 1) as it:
                        fetch(b, table, group, it, False)
                    group += NSLOT // STEP


def kernel(**inputs):
    import concourse.bacc as bacc
    from concourse.bass_utils import run_bass_kernel_spmd as run

    f = {k: np.asarray(a) for k, a in inputs.items()}
    vec = lambda name: f[name].reshape(-1)
    rows = np.concatenate([vec(n) for n in ("dt_bias", "a_log", "d_skip", "q_norm_w", "k_norm_w",
                                            "lambda_q1", "lambda_k1", "lambda_q2", "lambda_k2")])
    cols = np.concatenate([
        vec("mix_norm_w").reshape(8, P).T, vec("ssd_norm_w").reshape(4, P).T, vec("subln_w").reshape(1, P).T,
        f["conv_w"][0].T.reshape(CB, P, CONVW).transpose(1, 0, 2).reshape(P, CB * CONVW),
        vec("conv_b").reshape(CB, P).T], axis=1)
    inv = np.power(np.float32(500000.0), -np.arange(0, 16, 2, dtype=np.float32) / np.float32(16))
    ang = np.arange(SEQ, dtype=np.float32)[:, None] * inv[None, :].astype(np.float32)
    table = lambda t: t.astype(np.float32).reshape(NB, P, RD).transpose(1, 0, 2).reshape(P, NB * RD)
    consts = np.concatenate([np.eye(P, dtype=np.float32), np.triu(np.ones((P, P), np.float32)),
                             table(np.cos(ang)), table(np.sin(ang)),
                             np.broadcast_to(np.arange(NKEY, dtype=np.float32), (P, NKEY))], axis=1)
    arrays = {
        "x": f["x"][0], "w_in": f["w_in"][0], "w_out": f["w_out"][0], "w_q": f["peer_w_q"][0],
        "keys_t": f["peer_sub_keys"][0].reshape(2 * PH, NKEY, P).transpose(2, 0, 1),
        "u": f["peer_u"][0],
        "u_t": f["peer_u"][0].reshape(NKEY, NKEY, KC, P).transpose(1, 3, 2, 0).reshape(NKEY, P, DM), "v": f["peer_v"][0], "rows": np.broadcast_to(rows, (P, NROW)),
        "ffn_w": np.broadcast_to(vec("ffn_norm_w"), (P, DM)), "cols": cols, "consts": consts,
    }
    arrays = {k: np.ascontiguousarray(a) for k, a in arrays.items()}
    nc = bacc.Bacc("TRN2", target_bir_lowering=False, num_devices=1)
    args = [nc.dram_tensor(k, a.shape, F32, kind="ExternalInput").ap() for k, a in arrays.items()]
    args.append(nc.dram_tensor("out", (SEQ, DM), F32, kind="ExternalOutput").ap())
    block_program(nc, *args)
    r = run(nc, [arrays], core_ids=[0])
    return r.results[0]["out"].reshape(1, SEQ, DM)
```

```python
import math
import numpy as np
import concourse.bass as bass
from concourse import mybir
from contextlib import ExitStack

F32 = mybir.dt.float32
I32 = mybir.dt.int32
U32 = mybir.dt.uint32
ALU = mybir.AluOpType
ACT = mybir.ActivationFunctionType
AXX = mybir.AxisListType.X

P = 128
SEQ, DM = 512, 1024
NB = SEQ // P
KC = DM // P
HALF = 512
SSDW, HD, NH, NG, NST = 512, 64, 8, 2, 128
HPG = NH // NG
CONVW, CONVC = 4, 1024
CB = CONVC // P
DH, QKD, VD = 4, 64, 128
RD = 8
EPS = 1e-6
LAMBDA_INIT = 0.8 - 0.6 * math.exp(-0.3 * 0)
PH, TOPK, NKEY, NEXP = 8, 16, 128, 128 * 128
NSLOT = PH * TOPK
NEG = -3.0e38
NHALFW = 4
RING = 4
STEP = 8
NG_TOK = 4
HB = NB // 2
HT = HB * P
COL_Z, COL_XBC, COL_DT, COL_Q, COL_K, COL_V = 0, 512, 1536, 1544, 2056, 2568

R_DTB, R_ALOG, R_D, R_QN, R_KN, R_L = 0, 8, 16, 24, 88, 152
NROW = R_L + 4 * 64
C_ID, C_TRI, C_COS, C_SIN, C_IOTA = 0, 128, 256, 256 + NB * RD, 256 + 2 * NB * RD
NCONST = C_IOTA + NKEY
V_MIX, V_SSD, V_SUB, V_CW, V_CB = 0, 8, 12, 13, 13 + CB * CONVW
NCOLP = V_CB + CB


def bc(ap, axis, n):
    a = ap.unsqueeze(axis)
    shape = list(a.shape)
    shape[axis] = n
    return a.broadcast_to(shape)


def block_program(nc, x, w_in, w_out, w_q, keys_t, u, u_t, v, rows, ffn_w, cols, consts, out):
    ctx = ExitStack()
    with ctx:
        def sb(name, shape, dt=F32):
            return ctx.enter_context(nc.sbuf_tensor(name, shape, dt))

        def sem(name):
            return ctx.enter_context(nc.semaphore(name))

        X = sb("X", [P, NB, DM])
        Y = sb("Y", [P, NB, DM])
        T8 = sb("T8", [P, 2, KC, HT])
        BIG = sb("BIG", [P, 32832])
        place = [0]

        def part(n):
            place[0] += n
            return BIG[:, place[0] - n:place[0]]

        W = part(NHALFW * 4 * HALF).rearrange("p (a n) -> p a n", a=NHALFW)
        XBCF = part(CB * (SEQ + CONVW - 1))
        XBC = XBCF.rearrange("p (c n) -> p c n", c=CB)
        XC = part(CB * SEQ).rearrange("p (c n) -> p c n", c=CB)
        MID = part(4 * NB * HALF).rearrange("p (a b n) -> p a b n", a=4, b=NB)
        Z, Q, K, V = (MID[:, i] for i in range(4))
        QT = part(DH * SEQ).rearrange("p (h n) -> p h n", h=DH)
        KT = part(DH * SEQ).rearrange("p (h n) -> p h n", h=DH)
        MIX = part(4 * DM)
        DAB = MIX[:, 0:DM].rearrange("p (h n) -> p h n", n=P)
        SEG = MIX[:, DM:2 * DM].rearrange("p (g n) -> p g n", g=NG)
        PP = MIX[:, 2 * DM:4 * DM].rearrange("p (a j n) -> p a j n", a=2, j=2)
        GD = BIG[:, 0:HT * NKEY].rearrange("p (t j) -> p t j", j=NKEY)
        KEYS = K.rearrange("p b (a n) -> p (b a) n", n=NKEY)
        FW = MIX[:, 0:DM]
        ROWS = sb("ROWS", [P, NROW])
        COLS = sb("COLS", [P, NCOLP])
        CONST = sb("CONST", [P, NCONST])
        ONES = sb("ONES", [P, P])
        IDENT = CONST[:, C_ID:C_ID + P]
        TRI = CONST[:, C_TRI:C_TRI + P]
        SS = sb("SS", [P, 8 * NB])
        DT = sb("DT", [P, NB, NH])
        DTS = sb("DTS", [P, 6, NB * NH])
        DA = sb("DA", [P, NB, NH])
        ACS = sb("ACS", [P, NB, 2 * NH])
        EACS = sb("EACS", [P, NB, NH])
        DTE = sb("DTE", [P, NB, NH])
        CD = sb("CD", [P, NB, NH])
        AH = sb("AH", [P, NH])
        UV = sb("UV", [P, RING, DM])
        XS, XDT, XDTE = UV[:, 0, 0:SSDW], UV[:, 0, SSDW:DM], UV[:, 1, 0:SSDW]
        ST = UV[:, 1, SSDW:DM]
        BM = UV[:, 3, SEQ:SEQ + NG * NST]
        TMP = XBCF[:, 0:2 * HALF].rearrange("p (a n) -> p a n", a=2)
        AT = MIX[:, DM:DM + SEQ]
        CBM = UV[:, 3, SEQ + 256:DM].rearrange("p (g n) -> p g n", g=NG)
        SMALL = sb("SMALL", [P, 64])
        MX = sb("MX", [P, 2, 2])
        NMX = sb("NMX", [P, 2, 2])
        SUMS = sb("SUMS", [P, DH * NB, 2])
        RS = sb("RS", [P, DH])
        LAM = sb("LAM", [P, 6])
        LT = V[:, 3, 0:QKD]
        WC = sb("WC", [P, 8])
        OH = XBCF[:, 1024:2048].rearrange("p (a n) -> p a n", a=2)
        ISELS = XBCF[:, 2048:3072].rearrange("p (b j k) -> p b j k", b=NB, j=2)
        CAND = XBCF[:, 3072:3328]
        TOPS = XBCF[:, 3328:3456].rearrange("p (h k) -> p h k", k=TOPK)
        TOPIF = XBCF[:, 3456:3712].rearrange("p (h j k) -> p h j k", j=2, k=TOPK)
        PABF = XBCF[:, 3712:3968].rearrange("p (j k) -> p j k", j=2)
        POS = XBCF[:, 3968:4096].bitcast(U32).rearrange("p (h k) -> p h k", k=TOPK)
        TOPI = MIX[:, DM + SEQ:DM + SEQ + 256].bitcast(U32).rearrange("p (h j k) -> p h j k", j=2, k=TOPK)
        PAB = MIX[:, DM + SEQ + 256:2 * DM].bitcast(U32).rearrange("p (j k) -> p j k", j=2)
        TOPV = SMALL[:, 32:64].rearrange("p (j k) -> p j k", j=2)
        G = sb("G", [P, NB, NSLOT])
        IDX = sb("IDX", [P, HB, NSLOT], I32)
        IXC = sb("IXC", [P, 2, STEP], I32)
        H = sb("H", [P, NSLOT])
        GH = sb("GH", [P, NSLOT])
        KT3 = sb("KT3", [P, 3, HT])
        GE = sb("GE", [P, 2, HT])
        ONEHOT = Y[:, HB:NB, :].rearrange("p b (i a k) -> p b i a k", i=NG_TOK, a=2)
        UT = T8[:, 0, :, :].rearrange("p (q c) (h i) -> p q (c h) i", q=2, h=2)
        VT = Y[:, HB:NB, :]
        Q2 = XC.rearrange("p c (h n) -> p (c h) n", h=2)
        SC = [Z, Q, QT, KT]
        BANKS = ctx.enter_context(nc.psum_tensor("BANKS", [P, 8, HALF], F32))
        PS = [BANKS[:, i, :] for i in range(8)]

        ld_x = [sem(f"ld_x{i}") for i in range(NB)]
        ld_par, ld_fw, ld_keys = sem("ld_par"), sem("ld_fw"), sem("ld_keys")
        w_full = [sem(f"w_full{i}") for i in range(NHALFW)]
        sq_done, rs_half, rs_done, y_ready, t_full, t_done = (sem(n) for n in (
            "sq_done", "rs_half", "rs_done", "y_ready", "t_full", "t_done"))
        proj_full, proj_free, conv_done, xc_done = (sem(n) for n in (
            "proj_full", "proj_free", "conv_done", "xc_done"))
        dt_step, dt_act, da_ready = sem("dt_step"), sem("dt_act"), sem("da_ready")
        dab_ready, ssd_in, ssd_in_free, seg_full, seg_ready, seg_exp = (sem(n) for n in (
            "dab_ready", "ssd_in", "ssd_in_free", "seg_full", "seg_ready", "seg_exp"))
        m_ready, xdt_ready, y_full, yoff_full, st_full, y_free, st_ready = (sem(n) for n in (
            "m_ready", "xdt_ready", "y_full", "yoff_full", "st_full", "y_free", "st_ready"))
        qk_ready, qkt_full, qkt_done = sem("qk_ready"), sem("qkt_full"), sem("qkt_done")
        sc_full, mx_ready, exp_done, at_ready, att_full, att_done, pv_full, o_free = (sem(n) for n in (
            "sc_full", "mx_ready", "exp_done", "at_ready", "att_full", "att_done", "pv_full", "o_free"))
        ysq_ready, ysq_done, yrs_half, yrs_done = (sem(n) for n in (
            "ysq_ready", "ysq_done", "yrs_half", "yrs_done"))
        res_full, res_free = sem("res_full"), sem("res_free")
        q2_full, q2_done, ks_full, ks_done = (sem(n) for n in ("q2_full", "q2_done", "ks_full", "ks_done"))
        g_raw, g_exp, idx_ready = sem("g_raw"), sem("g_exp"), sem("idx_ready")
        ixc_ready, used, h_ready, gelu_done, out_ready, stored = (sem(n) for n in (
            "ixc_ready", "used", "h_ready", "gelu_done", "out_ready", "stored"))
        sel_ready, selt_full, selt_done, oh_ready, gb_full, gb_done = (sem(n) for n in (
            "sel_ready", "selt_full", "selt_done", "oh_ready", "gb_full", "gb_done"))
        u_in, v_in = [sem(f"u_in{i}") for i in range(2)], [sem(f"v_in{i}") for i in range(2)]
        hd_full, ge_done, yd_ready, vd_full = (sem(n) for n in ("hd_full", "ge_done", "yd_ready", "vd_full"))
        row_in = [sem(f"row_in{i}") for i in range(RING)]
        dve_seq, lam_step, lam_act = sem("dve_seq"), sem("lam_step"), sem("lam_act")

        tiles = ([(w_in, COL_XBC), (w_in, COL_XBC + HALF), (w_in, COL_Z), (w_in, COL_Q), (w_in, COL_K),
                  (w_in, COL_V)]
                 + 2 * ([(w_out, 0), (w_out, HALF)] + [(w_q, i * HALF) for i in range(4)]))
        products_of = ([(proj_full, k) for k in (5, 9, 14, 18, 22, 26)] + [(res_full, NB)] * 2
                       + [(q2_full, 4 * (i + 1)) for i in range(4)] + [(res_full, 2 * NB)] * 2
                       + [(q2_full, 2 * PH + 4 * (i + 1)) for i in range(2)])
        WDT = K[:, 0, 0:KC * NH]

        v_j = v.rearrange("(i j) n -> j i n", j=NKEY)

        QROWS, LAST = 12, 8
        QUADS = (NSLOT - LAST) // QROWS
        SEGPAIRS = 2 * QUADS + 1
        TAIL = NKEY // 2 - 3 * SEGPAIRS

        STEPS = [("z", 0), ("z", 1), ("S1", 0), ("z", 2), ("z", 3), ("S2", 0), ("q", 0), ("S3", 0), ("S1", 1),
                 ("q", 1), ("q", 2), ("S2", 1), ("q", 3), ("S3", 1), ("S1", 2), ("q1", 0), ("k", 0), ("k", 1),
                 ("S2", 2), ("k", 2), ("S3", 2), ("S1", 3), ("q2", 0), ("k", 3), ("v", 0), ("S2", 3), ("S3", 3),
                 ("k1", 0), ("v", 1), ("k2", 0), ("v", 2), ("v", 3)]
        HEADS = DH * NB
        on = lambda names, b: [(n, b) for n in names.split()]
        many = lambda name, first, end: [(name, i) for i in range(first, end)]
        after = {3: on("N", 0), 4: on("T", 0), 5: on("R0", 0), 6: on("R1 Q", 0), 7: on("F", 0) + on("N", 1),
                 8: on("U", 0) + on("T", 1), 9: on("R0 R1 Q", 1), 10: on("F U", 1), 11: on("N", 2) + many("W", 0, 4),
                 12: many("W", 4, 8), 13: many("W", 8, 12), 14: many("W", 12, 16) + many("K", 0, 4),
                 15: on("N", 3) + many("K", 4, 8) + many("r", 0, 1) + on("T", 2) + many("r", 1, 2) + on("R0", 2)
                 + many("r", 2, 3) + on("R1 Q", 2) + on("T", 3) + many("r", 3, 4) + on("R0", 3) + on("F", 2)
                 + many("r", 4, 5) + on("R1 Q", 3) + on("U", 2) + on("F U", 3)
                 + many("W", 16, 32) + many("K", 8, 16)
                 + many("r", 5, 8) + on("L", 0) + many("r", 8, 16) + on("L", 1)}
        ATT = [("A", 0), ("A", 1)]
        for i in range(HEADS):
            ATT.append(("B", i))
            if i + 2 < HEADS:
                ATT.append(("A", i + 2))
            ATT += [("C", i)] + after.get(i, [])
        norms = [s for s in ATT if s[0] in ("N", "F")]
        turns = [s for s in ATT if s[0] in ("T", "U")]

        def y_count(kind, b):
            return b + 1 if kind == 0 else NB + 1 + norms.index(("NF"[kind - 1], b))

        def t_count(kind, b):
            return 2 * b if kind == 0 else 2 * NB + 2 * turns.index(("TU"[kind - 1], b))

        block = ctx.enter_context(nc.Block())

        @block.sync
        def _(sp):
            for b in range(NB):
                sp.dma_start(X[:, b, :], x[b * P:(b + 1) * P, :]).then_inc(ld_x[b], 16)
                if b == 0:
                    sp.dma_start(CONST[:], consts).then_inc(ld_par, 16)
                    sp.dma_start(COLS[:], cols).then_inc(ld_par, 16)
                    sp.dma_start(ROWS[:], rows).then_inc(ld_par, 16)
                    sp.dma_start(WDT.rearrange("p (c n) -> p c n", n=NH),
                                 w_in[:, COL_DT:COL_DT + NH].rearrange("(c p) n -> p c n", p=P)).then_inc(ld_par, 16)
            n = 0
            for mat, c0 in tiles:
                if n == 16:
                    sp.wait_ge(y_free, 4 * NB)
                    sp.dma_start(FW, ffn_w).then_inc(ld_fw, 16)
                    sp.wait_ge(proj_full, 26 + 2 * NB)
                    sp.dma_start(KEYS, keys_t).then_inc(ld_keys, 16)
                for half in range(2):
                    if n >= NHALFW and half == 0:
                        sp.wait_ge(*products_of[n // 2 - 2])
                    src = mat[half * 4 * P:(half + 1) * 4 * P, c0:c0 + HALF].rearrange("(c p) n -> p c n", p=P)
                    sp.dma_start(W[:, n % NHALFW, :].rearrange("p (c n) -> p c n", n=HALF), src)\
                        .then_inc(w_full[n % NHALFW], 16)
                    n += 1

            def load_u(q, it):
                sp.dma_start(UT[:, q], u_t[bass.ds(it * 2 + q, 1)].rearrange("j p (c i) -> p (j c) i", c=KC))\
                    .then_inc(u_in[q], 16)

            def load_v(q, it):
                sp.dma_start(VT[:, q, :], v_j[bass.ds(it * 2 + q, 1)].rearrange("j p n -> p (j n)"))\
                    .then_inc(v_in[q], 16)

            sp.wait_ge(q2_full, 2 * PH)
            load_u(0, 0)
            load_u(1, 0)
            sp.wait_ge(gb_full, HT // NG_TOK)
            load_v(0, 0)
            load_v(1, 0)
            sp.wait_ge(hd_full, 1)
            load_u(0, 1)
            sp.wait_ge(hd_full, 2)
            load_u(1, 1)
            sp.wait_ge(vd_full, 1)
            load_v(0, 1)
            with sp.Fori(2, NKEY // 2, 1) as it:
                sp.wait_ge(hd_full, it * 2 - 1)
                load_u(0, it)
                sp.wait_ge(vd_full, it * 2 - 2)
                load_v(1, it - 1)
                sp.wait_ge(hd_full, it * 2)
                load_u(1, it)
                sp.wait_ge(vd_full, it * 2 - 1)
                load_v(0, it)
            sp.wait_ge(vd_full, NKEY - 2)
            load_v(1, NKEY // 2 - 1)
            for b in range(NB):
                sp.wait_ge(out_ready, b + 1)
                sp.dma_start(out[b * P:(b + 1) * P, :], X[:, b, :]).then_inc(stored, 16)
            sp.wait_ge(stored, 16 * NB)

        @block.tensor
        def _(pe):
            tile = [0]

            read_by = [(y_free, 4 * NB), (y_free, 4 * NB)]

            def bank_01(c, signal, count):
                pe.wait_ge(*read_by[c])
                read_by[c] = (signal, count)
                return PS[c]

            def transpose_block(kind, b):
                pe.wait_ge(y_ready, y_count(kind, b))
                for c in range(2):
                    j = t_count(kind, b) + c
                    if kind == 0:
                        bank = PS[j % 4]
                        if j >= 4:
                            pe.wait_ge(t_done, j - 3)
                    else:
                        bank = bank_01(c, t_done, j + 1)
                    for i in range(4):
                        last = nc.tensor.transpose(bank[:, i * P:(i + 1) * P],
                                                   Y[:, b, (4 * c + i) * P:(4 * c + i + 1) * P], IDENT)
                    last.then_inc(t_full, 1)

            def weights_in():
                n = tile[0]
                tile[0] += 2
                for half in range(2):
                    pe.wait_ge(w_full[(n + half) % NHALFW], 16 * ((n + half) // NHALFW + 1))
                return n

            job = [0]

            def next_bank():
                j = job[0]
                job[0] += 1
                if j >= 4:
                    pe.wait_ge(proj_free, j - 3)
                return PS[4 + j % 4]

            pe.wait_ge(ld_par, 64)
            for b in range(NB):
                transpose_block(0, b)
            pe.wait_ge(t_done, 2 * NB)

            bank = next_bank()
            for b in range(NB):
                for c in range(KC):
                    last = nc.tensor.matmul(bank[:, b * NH:(b + 1) * NH], T8[:, b // 2, c, b % 2 * P:(b % 2 + 1) * P],
                                            WDT[:, c * NH:(c + 1) * NH], start=(c == 0), stop=(c == KC - 1))
            last.then_inc(proj_full, 1)
            for tl in range(2):
                n = weights_in()
                for cb in range(4):
                    bank = next_bank()
                    for c in range(KC):
                        wt = W[:, (n + c // 4) % NHALFW, (c % 4) * HALF + cb * P:(c % 4) * HALF + (cb + 1) * P]
                        last = nc.tensor.matmul(bank[:, :], wt, T8[:, :, c, :], start=(c == 0), stop=(c == KC - 1))
                    last.then_inc(proj_full, 1)
            pe.wait_ge(da_ready, 1)
            bank = next_bank()
            for b in range(NB):
                nc.tensor.matmul(bank[:, b * 16:b * 16 + NH], TRI, DA[:, b, :], start=True, stop=True)
                last = nc.tensor.matmul(bank[:, b * 16 + NH:b * 16 + 16], ONES[:, :], DA[:, b, :],
                                        start=True, stop=True)
            last.then_inc(proj_full, 1)

            def ssd_maps(b):
                tok = slice(b * P, (b + 1) * P)
                if b:
                    pe.wait_ge(y_free, 4 * b)
                if b == 0:
                    pe.wait_ge(xc_done, CB)
                    pe.wait_ge(t_done, 2 * NB)
                for i in range(4):
                    last = nc.tensor.transpose(PS[0][:, i * P:(i + 1) * P], XC[:, i, tok], IDENT)
                last.then_inc(ssd_in, 1)
                for g in range(NG):
                    nc.tensor.transpose(PS[1][:, g * P:(g + 1) * P], XC[:, 4 + g, tok], IDENT)
                for g in range(NG):
                    last = nc.tensor.matmul(PS[1][:, (2 + g) * P:(3 + g) * P], XC[:, 4 + g, tok],
                                            XC[:, 6 + g, tok], start=True, stop=True)
                last.then_inc(ssd_in, 1)
                pe.wait_ge(dab_ready, b + 1)
                for g in range(NG):
                    if g:
                        pe.wait_ge(seg_ready, b * NG + g)
                    for h in range(HPG):
                        last = nc.tensor.matmul(PS[2][:, h * P:(h + 1) * P], DAB[:, g * HPG + h, :], TRI,
                                                start=True, stop=True)
                    last.then_inc(seg_full, 1)

            def ssd_products(b):
                tok = slice(b * P, (b + 1) * P)
                pe.wait_ge(m_ready, b * NG + NG)
                pe.wait_ge(xdt_ready, 2 * b + 1)
                pe.wait_ge(ssd_in_free, 3 * b + 1)
                for h in range(NH):
                    last = nc.tensor.matmul(PS[0][:, h * HD:(h + 1) * HD],
                                            SEG[:, h // HPG, (h % HPG) * P:(h % HPG + 1) * P],
                                            XDT[:, h * HD:(h + 1) * HD], start=True, stop=True)
                last.then_inc(y_full, 1)
                pe.wait_ge(seg_ready, b * NG + NG)
                if b:
                    pe.wait_ge(st_ready, b)
                    for g in range(NG):
                        last = nc.tensor.matmul(PS[2][:, g * 256:(g + 1) * 256], XC[:, 6 + g, tok],
                                                ST[:, g * 256:(g + 1) * 256], start=True, stop=True)
                    last.then_inc(yoff_full, 1)
                pe.wait_ge(ssd_in_free, 3 * b + 3)
                pe.wait_ge(xdt_ready, 2 * b + 2)
                for g in range(NG):
                    last = nc.tensor.matmul(PS[1][:, g * 256:(g + 1) * 256], BM[:, g * P:(g + 1) * P],
                                            XDTE[:, g * 256:(g + 1) * 256], start=True, stop=True)
                last.then_inc(st_full, 1)

            for step, b in STEPS:
                if step in ("z", "q", "k", "v"):
                    if b == 0:
                        n = weights_in()
                    bank = next_bank()
                    for c in range(KC):
                        wt = W[:, (n + c // 4) % NHALFW, (c % 4) * HALF:(c % 4 + 1) * HALF]
                        last = nc.tensor.matmul(bank[:, :], T8[:, b // 2, c, b % 2 * P:(b % 2 + 1) * P], wt,
                                                start=(c == 0), stop=(c == KC - 1))
                    last.then_inc(proj_full, 1)
                elif step == "S1":
                    ssd_maps(b)
                elif step == "S2":
                    ssd_products(b)
            for i, src in enumerate((Q, K)):
                for b in range(NB):
                    pe.wait_ge(qk_ready, i * NB + b + 1)
                    bank = next_bank()
                    for h in range(DH):
                        last = nc.tensor.transpose(bank[:, h * P:(h + 1) * P], src[:, b, h * P:(h + 1) * P], IDENT)
                    last.then_inc(proj_full, 1)

            pe.wait_ge(proj_free, job[0])

            def scores(b, h):
                i = b * DH + h
                if i >= 2:
                    pe.wait_ge(exp_done, 2 * (i - 1))
                for j in range(2):
                    last = nc.tensor.matmul(PS[4 + 2 * (i % 2) + j][:, 0:P * (b + 1)],
                                            QT[j * QKD:(j + 1) * QKD, h, b * P:(b + 1) * P],
                                            KT[j * QKD:(j + 1) * QKD, h, 0:P * (b + 1)], start=True, stop=True)
                    last.then_inc(sc_full, 1)

            def transpose_map(b, h):
                i = b * DH + h
                pe.wait_ge(at_ready, i + 1)
                if i >= 1:
                    pe.wait_ge(att_done, i)
                for kb in range(b + 1):
                    last = nc.tensor.transpose(PS[3][:, kb * P:(kb + 1) * P],
                                               PP[:, i % 2, 0, kb * P:(kb + 1) * P], IDENT)
                last.then_inc(att_full, 1)

            def values(b, h):
                i = b * DH + h
                pe.wait_ge(att_done, i + 1)
                if i == 0:
                    pe.wait_ge(y_free, 4 * NB)
                elif h == 0:
                    pe.wait_ge(o_free, b)
                for kb in range(b + 1):
                    last = nc.tensor.matmul(PS[2][:, h * P:(h + 1) * P], AT[:, kb * P:(kb + 1) * P],
                                            V[:, kb, h * P:(h + 1) * P], start=(kb == 0), stop=(kb == b))
                last.then_inc(pv_full, 1)

            for step, i in ATT:
                if step == "A":
                    scores(i // DH, i % DH)
                elif step == "B":
                    transpose_map(i // DH, i % DH)
                elif step == "C":
                    values(i // DH, i % DH)
                elif step == "T":
                    transpose_block(1, i)
                elif step == "U":
                    transpose_block(2, i)
                elif step in ("R0", "R1"):
                    c0 = int(step[1])
                    if i % 2 == 0:
                        weights_in()
                    n = 2 * c0
                    pe.wait_ge(t_done, t_count(1, i) + 2)
                    bank = bank_01(c0, res_free, 2 * i + c0 + 1)
                    for c in range(KC):
                        wt = W[:, (n + c // 4) % NHALFW, (c % 4) * HALF:(c % 4 + 1) * HALF]
                        last = nc.tensor.matmul(bank[:, :], T8[:, i // 2, c, i % 2 * P:(i % 2 + 1) * P], wt,
                                                start=(c == 0), stop=(c == KC - 1))
                    last.then_inc(res_full, 1)
                elif step == "W":
                    half, j = i // (2 * PH), i % (2 * PH)
                    if j == 0:
                        pe.wait_ge(t_done, t_count(2, 2 * half + 1) + 2)
                    if j % 4 == 0:
                        n = weights_in()
                    bank = bank_01(j % 2, q2_done, i + 1)
                    for c in range(KC):
                        wt = W[:, (n + c // 4) % NHALFW, (c % 4) * HALF + (j % 4) * P:(c % 4) * HALF + (j % 4 + 1) * P]
                        last = nc.tensor.matmul(bank[:, 0:HT], wt, T8[:, half, c, :],
                                                start=(c == 0), stop=(c == KC - 1))
                    last.then_inc(q2_full, 1)
                elif step == "K":
                    b, c = i // 4, i % 4
                    pe.wait_ge(q2_done, 2 * PH * (b // 2 + 1))
                    pe.wait_ge(ld_keys, 16)
                    bank = bank_01(c % 2, ks_done, i + 1)
                    for k in range(4):
                        hj = 4 * c + k
                        last = nc.tensor.matmul(bank[:, k * P:(k + 1) * P], Q2[:, hj, b % 2 * P:(b % 2 + 1) * P],
                                                KEYS[:, hj, :], start=True, stop=True)
                    last.then_inc(ks_full, 1)

            for n, b in enumerate(range(HB, NB)):
                pe.wait_ge(sel_ready, n + 1)
                pe.wait_ge(ks_done, 4 * NB)
                for a, src in enumerate((ISELS[:, b, 0, :], ISELS[:, b, 1, :], G[:, b, :])):
                    last = nc.tensor.transpose(PS[4 + n][:, a * P:(a + 1) * P], src, IDENT)
                last.then_inc(selt_full, 1)

            def weights_of_tokens(it, first):
                for q in range(2):
                    pe.wait_ge(oh_ready, it * 2 + (q + 1))
                    if not first:
                        pe.wait_ge(gb_done, it * 2 + (q - 1))
                    for i in range(NG_TOK):
                        last = nc.tensor.matmul(PS[2 + q][:, i * P:(i + 1) * P], ONEHOT[:, q, i, 0, :],
                                                ONEHOT[:, q, i, 1, :], start=True, stop=True)
                    last.then_inc(gb_full, 1)

            weights_of_tokens(0, True)
            with pe.Fori(1, HT // NG_TOK // 2, 1) as it:
                weights_of_tokens(it, False)

            def hidden(q, it, first):
                pe.wait_ge(u_in[q], it * 16 + 16)
                if not first:
                    pe.wait_ge(ge_done, it * 2 + (q - 1))
                for c in range(KC):
                    last = nc.tensor.matmul(PS[q][:, 0:HT], UT[:, q, c, :], T8[:, 1, c, :],
                                            start=(c == 0), stop=(c == KC - 1))
                last.then_inc(hd_full, 1)

            def products(q, it, first=False, final=False):
                pe.wait_ge(v_in[q], it * 16 + 16)
                pe.wait_ge(yd_ready, it * 2 + (q + 1))
                for t in range(HB):
                    for n in range(2):
                        last = nc.tensor.matmul(PS[4 + 2 * t + n][:, :], GE[:, q, t * P:(t + 1) * P],
                                                VT[:, q, n * HALF:(n + 1) * HALF], start=first, stop=final,
                                                skip_group_check=True)
                last.then_inc(vd_full, 1)

            hidden(0, 0, True)
            hidden(1, 0, True)
            pe.wait_ge(selt_done, HB)
            products(0, 0, first=True)
            with pe.Fori(1, NKEY // 2, 1) as it:
                hidden(0, it, False)
                products(1, it - 1)
                hidden(1, it, False)
                products(0, it)
            products(1, NKEY // 2 - 1, final=True)

        @block.scalar
        def _(act):
            for b in range(NB):
                act.wait_ge(ld_x[b], 16)
                nc.scalar.activation(Y[:, b, :], X[:, b, :], ACT.Square, accum_out=SS[:, b:b + 1]).then_inc(sq_done, 1)
            act.wait_ge(rs_half, 1)
            nc.scalar.activation(SS[:, 0:NB], SS[:, 0:NB], ACT.Sqrt).then_inc(rs_done, 1)
            job = [0]

            def drain_bank(dst, func=ACT.Copy, view=None):
                j = job[0]
                job[0] += 1
                act.wait_ge(proj_full, j + 1)
                src = PS[4 + j % 4][:, :] if view is None else view(PS[4 + j % 4])
                nc.scalar.activation(dst, src, func).then_inc(proj_free, 1)

            drain_bank(DT[:, :, :].rearrange("p b h -> p (b h)"), view=lambda t: t[:, 0:NB * NH])
            act.wait_ge(dt_step, 1)
            nc.scalar.activation(DTS[:, 1], DTS[:, 0], ACT.Exp, scale=-1.0).then_inc(dt_act, 1)
            act.wait_ge(dt_step, 2)
            nc.scalar.activation(DTS[:, 3], DTS[:, 2], ACT.Ln).then_inc(dt_act, 1)
            nc.scalar.activation(AH[:, :], ROWS[:, R_ALOG:R_ALOG + NH], ACT.Exp).then_inc(dt_act, 1)
            act.wait_ge(lam_step, 2)
            nc.scalar.activation(LAM[:, 2:4], LAM[:, 0:2], ACT.Exp).then_inc(lam_act, 1)
            for cb in range(CB + 1):
                if cb < CB:
                    drain_bank(XBC[:, cb, CONVW - 1:])
                else:
                    drain_bank(ACS[:, :, :].rearrange("p b h -> p (b h)"), view=lambda t: t[:, 0:NB * 2 * NH])
                if cb:
                    act.wait_ge(conv_done, cb)
                    nc.scalar.activation(XC[:, cb - 1, :], XC[:, cb - 1, :], ACT.Silu,
                                         bias=COLS[:, V_CB + cb - 1:V_CB + cb]).then_inc(xc_done, 1)
            act.wait_ge(proj_free, 10)
            nc.scalar.activation(EACS[:, :, :], ACS[:, :, 0:NH], ACT.Exp).then_inc(dt_act, 1)
            nc.scalar.activation(CD[:, :, :], ACS[:, :, NH:2 * NH], ACT.Exp).then_inc(dt_act, 1)
            act.wait_ge(dt_step, 3)
            nc.scalar.activation(DTE[:, :, :], DTE[:, :, :], ACT.Exp).then_inc(dt_act, 1)
            for step, b in STEPS:
                if step == "z":
                    drain_bank(Z[:, b, :], ACT.Silu)
                elif step in ("q", "k", "v"):
                    drain_bank({"q": Q, "k": K, "v": V}[step][:, b, :])
                elif step in ("q1", "k1"):
                    act.wait_ge(yrs_half, 1 if step == "q1" else 2)
                    nc.scalar.activation(SS[:, 0:8 * NB], SS[:, 0:8 * NB], ACT.Sqrt).then_inc(yrs_done, 1)
                elif step == "S1":
                    if b:
                        act.wait_ge(y_free, 4 * b)
                        act.wait_ge(st_full, b)
                    act.wait_ge(ssd_in, 2 * b + 1)
                    nc.scalar.activation(XS[:, :], PS[0][:, :], ACT.Copy).then_inc(ssd_in_free, 1)
                    act.wait_ge(ssd_in, 2 * b + 2)
                    nc.scalar.activation(BM[:, :], PS[1][:, 0:NG * P], ACT.Copy).then_inc(ssd_in_free, 1)
                    for g in range(NG):
                        act.wait_ge(seg_ready, b * NG + g + 1)
                        nc.scalar.activation(SEG[:, g, :], SEG[:, g, :], ACT.Exp).then_inc(seg_exp, 1)
            for dst in (QT, KT):
                for b in range(NB):
                    drain_bank(dst[:, :, b * P:(b + 1) * P], view=lambda t: t[:, :].rearrange("p (h n) -> p h n", n=P))

            def exps(b, h):
                i = b * DH + h
                act.wait_ge(mx_ready, i + 1)
                if i >= 2:
                    act.wait_ge(att_full, i - 1)
                for j in range(2):
                    nc.scalar.activation(PP[:, i % 2, j, 0:P * (b + 1)], PS[4 + 2 * (i % 2) + j][:, 0:P * (b + 1)],
                                         ACT.Exp, bias=NMX[:, i % 2, j:j + 1], scale=QKD ** -0.5,
                                         accum_out=SUMS[:, i, j:j + 1]).then_inc(exp_done, 1)

            for step, i in ATT:
                if step == "A":
                    exps(i // DH, i % DH)
                elif step == "B":
                    b = i // DH
                    act.wait_ge(att_full, i + 1)
                    if i:
                        act.wait_ge(pv_full, i)
                    nc.scalar.activation(AT[:, 0:P * (b + 1)], PS[3][:, 0:P * (b + 1)], ACT.Copy)\
                        .then_inc(att_done, 1)
                elif step == "N":
                    act.wait_ge(yrs_half, 2 + i + 1)
                    nc.scalar.activation(SMALL[:, 0:6], SMALL[:, 0:6], ACT.Sqrt).then_inc(yrs_done, 1)
                elif step == "Q":
                    act.wait_ge(res_free, 2 * i + 2)
                    act.wait_ge(t_full, t_count(1, i) + 2)
                    nc.scalar.activation(Y[:, i, :], X[:, i, :], ACT.Square,
                                         accum_out=SS[:, i:i + 1]).then_inc(sq_done, 1)
                elif step == "F":
                    act.wait_ge(rs_half, 2 + i)
                    nc.scalar.activation(SS[:, i:i + 1], SS[:, i:i + 1], ACT.Sqrt).then_inc(rs_done, 1)
                elif step == "W":
                    act.wait_ge(q2_full, i + 1)
                    if i == 2 * PH:
                        act.wait_ge(ks_full, 4 * HB)
                    nc.scalar.activation(Q2[:, i % (2 * PH), :], PS[i % 2][:, 0:HT], ACT.Copy).then_inc(q2_done, 1)
                elif step == "K":
                    act.wait_ge(ks_full, i + 1)
                    nc.scalar.activation(SC[i // 4][:, i % 4, :], PS[i % 2][:, :], ACT.Copy).then_inc(ks_done, 1)

            for b in range(NB):
                act.wait_ge(g_raw, b + 1)
                nc.scalar.activation(G[:, b, :], G[:, b, :], ACT.Exp).then_inc(g_exp, 1)
                if b >= HB:
                    act.wait_ge(selt_full, b - HB + 1)
                    nc.scalar.activation(KT3[:, :, (b - HB) * P:(b - HB + 1) * P],
                                         PS[4 + b - HB][:, 0:3 * P].rearrange("p (a n) -> p a n", a=3), ACT.Copy)\
                        .then_inc(selt_done, 1)
            with act.Fori(0, HT // NG_TOK // 2, 1) as it:
                for q in range(2):
                    act.wait_ge(gb_full, it * 2 + (q + 1))
                    nc.scalar.activation(GD[:, bass.ds((it * 2 + q) * NG_TOK, NG_TOK), :],
                                         PS[2 + q][:, :].rearrange("p (t j) -> p t j", j=NKEY), ACT.Copy)\
                        .then_inc(gb_done, 1)

            def gelus(it, first):
                for q in range(2):
                    act.wait_ge(hd_full, it * 2 + (q + 1))
                    if not first:
                        act.wait_ge(vd_full, it * 2 + (q - 1))
                    nc.scalar.activation(GE[:, q, :], PS[q][:, 0:HT], ACT.Gelu).then_inc(ge_done, 1)

            def gelu_of_rows(b):
                act.wait_ge(h_ready, b + 1)
                nc.scalar.activation(H[:, :], H[:, :], ACT.Gelu).then_inc(gelu_done, 1)

            gelu_of_rows(0)
            gelus(0, True)
            with act.Fori(1, 2 * SEGPAIRS, 1) as it:
                gelus(it, False)
            gelu_of_rows(1)
            with act.Fori(2 * SEGPAIRS, NKEY // 2, 1) as it:
                gelus(it, False)

        @block.vector
        def _(dve):
            seq = [0]

            def link(ins):
                seq[0] += 1
                ins.then_inc(dve_seq, 1)
                dve.wait_ge(dve_seq, seq[0])

            tt, ts, stt = nc.vector.tensor_tensor, nc.vector.tensor_scalar, nc.vector.scalar_tensor_tensor

            def inverse_mean(dst, src, n):
                link(ts(dst, src, 1.0 / n, EPS, ALU.mult, ALU.add))
                return nc.vector.reciprocal(dst, dst)

            def evacuate_transposes(kind, b):
                for c in range(2):
                    j = t_count(kind, b) + c
                    dve.wait_ge(t_full, j + 1)
                    src = PS[j % 4 if kind == 0 else c][:, :].rearrange("p (i n) -> p i n", n=P)
                    dst = T8[:, b // 2, 4 * c:4 * c + 4, b % 2 * P:(b % 2 + 1) * P]
                    if kind == 0:
                        w = COLS[:, V_MIX + 4 * c:V_MIX + 4 * c + 4]
                        tt(dst, src, bc(w, 2, P), ALU.mult).then_inc(t_done, 1)
                    elif kind == 1:
                        tt(dst, src, bc(WC[:, 4 * c:4 * c + 4], 2, P), ALU.mult).then_inc(t_done, 1)
                    else:
                        nc.vector.tensor_copy(dst, src).then_inc(t_done, 1)

            nc.vector.memset(ONES[:, :], 1.0)
            nc.vector.memset(XBC[:, :, 0:CONVW - 1], 0.0)
            link(nc.vector.memset(ST[:, :], 0.0))
            dve.wait_ge(ld_par, 64)
            nc.vector.tensor_copy(WC[:, 0:4], COLS[:, V_SSD:V_SSD + 4])
            link(ts(WC[:, 4:8], COLS[:, V_SUB:V_SUB + 1].broadcast_to([P, 4]), 1.0 - LAMBDA_INIT, None, ALU.mult))
            dve.wait_ge(sq_done, NB)
            inverse_mean(SS[:, 0:NB], SS[:, 0:NB], DM).then_inc(rs_half, 1)
            dve.wait_ge(rs_done, 1)
            for b in range(NB):
                ts(Y[:, b, :], X[:, b, :], SS[:, b:b + 1], None, ALU.mult).then_inc(y_ready, 1)
            for b in range(NB):
                evacuate_transposes(0, b)

            dt = DT[:, :, :].rearrange("p b h -> p (b h)")
            dve.wait_ge(proj_free, 1)
            link(tt(DT[:, :, :], DT[:, :, :], bc(ROWS[:, R_DTB:R_DTB + NH], 1, NB), ALU.add))
            stt(DTS[:, 0], dt, -1.0, dt, ALU.mult, ALU.max).then_inc(dt_step, 1)
            dve.wait_ge(dt_act, 1)
            ts(DTS[:, 2], DTS[:, 1], 1.0, None, ALU.add).then_inc(dt_step, 1)
            dve.wait_ge(dt_act, 2)
            link(ts(DTS[:, 4], DTS[:, 2], 1.0, None, ALU.is_equal))
            link(tt(DTS[:, 3], DTS[:, 3], DTS[:, 4], ALU.add))
            link(stt(DTS[:, 5], DTS[:, 2], -1.0, DTS[:, 4], ALU.add, ALU.add))
            link(nc.vector.reciprocal(DTS[:, 5], DTS[:, 5]))
            link(tt(DTS[:, 3], DTS[:, 3], DTS[:, 5], ALU.mult))
            link(tt(DTS[:, 3], DTS[:, 3], DTS[:, 1], ALU.mult))
            link(stt(dt, dt, 0.0, DTS[:, 3], ALU.max, ALU.add))
            dve.wait_ge(dt_act, 3)
            stt(DA[:, :, :], DT[:, :, :], -1.0, bc(AH[:, :], 1, NB), ALU.mult, ALU.mult).then_inc(da_ready, 1)
            for i in range(2):
                a = ROWS[:, R_L + 128 * i:R_L + 128 * i + QKD]
                c = ROWS[:, R_L + 128 * i + QKD:R_L + 128 * i + 128]
                link(stt(LT, a, 1.0, c, ALU.mult, ALU.mult))
                nc.vector.reduce_sum(LAM[:, i:i + 1], LT, AXX).then_inc(lam_step, 1)
                dve.wait_ge(lam_step, i + 1)
            dve.wait_ge(lam_act, 1)
            link(tt(LAM[:, 4:5], LAM[:, 2:3], LAM[:, 3:4], ALU.subtract))
            link(ts(LAM[:, 4:5], LAM[:, 4:5], LAMBDA_INIT, -1.0, ALU.add, ALU.mult))

            for cb in range(CB):
                dve.wait_ge(proj_free, 2 + cb)
                w = lambda k: COLS[:, V_CW + cb * CONVW + k:V_CW + cb * CONVW + k + 1]
                link(ts(XC[:, cb, :], XBC[:, cb, 0:SEQ], w(0), None, ALU.mult))
                for k in range(1, CONVW):
                    ins = stt(XC[:, cb, :], XBC[:, cb, k:k + SEQ], w(k), XC[:, cb, :], ALU.mult, ALU.add)
                    if k < CONVW - 1:
                        link(ins)
                ins.then_inc(conv_done, 1)

            dve.wait_ge(proj_free, 10)
            tt(DTE[:, :, :], ACS[:, :, NH:2 * NH], ACS[:, :, 0:NH], ALU.subtract).then_inc(dt_step, 1)

            def head_squares(i, src, first):
                for b in range(NB):
                    dve.wait_ge(proj_free, first + b)
                    link(tt(TMP[:, 0, :], src[:, b, :], src[:, b, :], ALU.mult))
                    link(nc.vector.reduce_sum(SS[:, 8 * b:8 * b + 8],
                                              TMP[:, 0, :].rearrange("p (g d) -> p g d", d=QKD), AXX))
                inverse_mean(SS[:, 0:8 * NB], SS[:, 0:8 * NB], QKD).then_inc(yrs_half, 1)

            def norm_and_rotate(i, src):
                nw = ROWS[:, (R_QN, R_KN)[i]:(R_QN, R_KN)[i] + QKD]
                dve.wait_ge(yrs_done, i + 1)
                for b in range(NB):
                    h3 = src[:, b, :].rearrange("p (g d) -> p g d", d=QKD)
                    link(tt(h3, h3, bc(SS[:, 8 * b:8 * b + 8], 2, QKD), ALU.mult))
                    link(tt(h3, h3, bc(nw, 1, 8), ALU.mult))
                    cos = bc(CONST[:, C_COS + b * RD:C_COS + (b + 1) * RD], 1, 8)
                    sin = bc(CONST[:, C_SIN + b * RD:C_SIN + (b + 1) * RD], 1, 8)
                    t = [TMP[:, 1, 64 * k:64 * k + 64].rearrange("p (g d) -> p g d", d=RD) for k in range(4)]
                    tt(t[0], h3[:, :, 0:RD], cos, ALU.mult)
                    tt(t[1], h3[:, :, RD:2 * RD], sin, ALU.mult)
                    tt(t[2], h3[:, :, 0:RD], sin, ALU.mult)
                    link(tt(t[3], h3[:, :, RD:2 * RD], cos, ALU.mult))
                    tt(h3[:, :, 0:RD], t[0], t[1], ALU.subtract)
                    tt(h3[:, :, RD:2 * RD], t[2], t[3], ALU.add).then_inc(qk_ready, 1)
                    dve.wait_ge(qk_ready, i * NB + b + 1)

            hd3 = lambda ap: ap.rearrange("p (h d) -> p h d", d=HD)
            for step, b in STEPS:
                if step == "q1":
                    head_squares(0, Q, 15)
                elif step == "k1":
                    head_squares(1, K, 19)
                elif step == "q2":
                    norm_and_rotate(0, Q)
                elif step == "k2":
                    norm_and_rotate(1, K)
                elif step == "S1":
                    if b:
                        dve.wait_ge(seg_full, NG * b)
                        dve.wait_ge(st_full, b)
                    nc.vector.tensor_copy(DAB[:, :, :], bc(DA[:, b, :], 2, P)).then_inc(dab_ready, 1)
                    for g in range(NG):
                        dve.wait_ge(seg_full, NG * b + g + 1)
                        for h in range(HPG):
                            hh = g * HPG + h
                            last = ts(SEG[:, g, h * P:(h + 1) * P], PS[2][:, h * P:(h + 1) * P],
                                      ACS[:, b, hh:hh + 1], 0.0, ALU.subtract, ALU.min)
                        last.then_inc(seg_ready, 1)
                    dve.wait_ge(ssd_in_free, 3 * b + 2)
                    tt(CBM[:, :, :], PS[1][:, NG * P:2 * NG * P].rearrange("p (g n) -> p g n", n=P),
                       bc(TRI, 1, NG), ALU.mult).then_inc(ssd_in_free, 1)
                    dve.wait_ge(ssd_in_free, 3 * b + 3)
                    tt(hd3(XDT[:, :]), hd3(XS[:, :]), bc(DT[:, b, :], 2, HD), ALU.mult).then_inc(xdt_ready, 1)
                    dve.wait_ge(xdt_ready, 2 * b + 1)
                    dve.wait_ge(dt_act, 6)
                    tt(hd3(XDTE[:, :]), hd3(XDT[:, :]), bc(DTE[:, b, :], 2, HD), ALU.mult).then_inc(xdt_ready, 1)
                    for g in range(NG):
                        dve.wait_ge(seg_exp, NG * b + g + 1)
                        m = SEG[:, g, :].rearrange("p (h n) -> p h n", n=P)
                        tt(m, m, bc(CBM[:, g, :], 1, HPG), ALU.mult).then_inc(m_ready, 1)
                elif step == "S2":
                    y = Y[:, b, 0:SSDW]
                    link(tt(hd3(y), hd3(XS[:, :]), bc(ROWS[:, R_D:R_D + NH], 2, HD), ALU.mult))
                    dve.wait_ge(y_full, b + 1)
                    tt(y, y, PS[0][:, :], ALU.add).then_inc(y_free, 1)
                    dve.wait_ge(y_free, 4 * b + 1)
                    if b:
                        dve.wait_ge(yoff_full, b)
                        link(tt(hd3(TMP[:, 0, :]), hd3(PS[2][:, :]), bc(EACS[:, b, :], 2, HD), ALU.mult))
                        tt(y, y, TMP[:, 0, :], ALU.add).then_inc(y_free, 1)
                    else:
                        nc.vector.tensor_copy(TMP[:, 0, 0:2], TMP[:, 0, 2:4]).then_inc(y_free, 1)
                    dve.wait_ge(y_free, 4 * b + 2)
                elif step == "S3":
                    dve.wait_ge(st_full, b + 1)
                    link(tt(hd3(ST[:, :]), hd3(ST[:, :]), bc(CD[:, b, :], 2, HD), ALU.mult))
                    tt(ST[:, :], ST[:, :], PS[1][:, :], ALU.add).then_inc(st_ready, 1)
                    dve.wait_ge(st_ready, b + 1)
                    y = Y[:, b, 0:SSDW]
                    link(tt(y, y, Z[:, b, :], ALU.mult))
                    tt(TMP[:, 0, :], y, y, ALU.mult).then_inc(y_free, 1)
                    dve.wait_ge(y_free, 4 * b + 3)
                    nc.vector.reduce_sum(SMALL[:, 16 + NG * b:16 + NG * (b + 1)],
                                         TMP[:, 0, :].rearrange("p (g d) -> p g d", g=NG), AXX)\
                        .then_inc(y_free, 1)
                    dve.wait_ge(y_free, 4 * b + 4)
            def top16(rows):
                for vals, values, places in rows:
                    last = nc.vector.max(values[:, 0:8], vals)
                link(last)
                for vals, values, places in rows:
                    nc.vector.max_index(places[:, 0:8], values[:, 0:8], vals)
                for vals, values, places in rows:
                    last = nc.vector.match_replace(vals, values[:, 0:8], vals, NEG)
                link(last)
                for vals, values, places in rows:
                    last = nc.vector.max(values[:, 8:16], vals)
                link(last)
                for vals, values, places in rows:
                    last = nc.vector.max_index(places[:, 8:16], values[:, 8:16], vals)
                link(last)

            def choose(b, h):
                dve.wait_ge(ks_done, 4 * b + h // 2 + 1)
                sc = SC[b].rearrange("p a (i n) -> p (a i) n", n=NKEY)
                top16([(sc[:, 2 * h + j, :], TOPV[:, j, :], TOPI[:, h, j, :]) for j in range(2)])
                link(tt(CAND.rearrange("p (a c) -> p a c", c=TOPK), bc(TOPV[:, 0, :], 2, TOPK),
                        bc(TOPV[:, 1, :], 1, TOPK), ALU.add))
                top16([(CAND, TOPS[:, h, :], POS[:, h, :])])

            def keys_of_choice(b):
                tt(G[:, b, :].rearrange("p (h k) -> p h k", k=TOPK), TOPS[:, :, :],
                   TOPS[:, :, 0:1].broadcast_to([P, PH, TOPK]), ALU.subtract).then_inc(g_raw, 1)
                pos = POS[:, :, :].rearrange("p h k -> p (h k)")
                ts(PAB[:, 0, :], pos, 4, None, ALU.logical_shift_right)
                link(ts(PAB[:, 1, :], pos, 15, None, ALU.bitwise_and))
                nc.vector.tensor_copy(PABF[:, :, :], PAB[:, :, :])
                link(nc.vector.tensor_copy(TOPIF[:, :, :, :], TOPI[:, :, :, :]))
                for j in range(2):
                    for q in range(4):
                        oh = OH[:, q % 2, :].rearrange("p (k c) -> p k c", c=TOPK)
                        ph = PABF[:, j, 32 * q:32 * q + 32]
                        link(tt(oh, bc(CONST[:, C_IOTA:C_IOTA + TOPK], 1, 32), bc(ph, 2, TOPK), ALU.is_equal))
                        for h2 in range(2):
                            o = OH[:, q % 2, h2 * 256:(h2 + 1) * 256].rearrange("p (k c) -> p k c", c=TOPK)
                            last = tt(o, o, bc(TOPIF[:, 2 * q + h2, j, :], 1, TOPK), ALU.mult)
                        link(last)
                        link(nc.vector.reduce_sum(ISELS[:, b, j, 32 * q:32 * q + 32], oh, AXX))
                if b < HB:
                    stt(IDX[:, b, :], ISELS[:, b, 0, :], float(NKEY), ISELS[:, b, 1, :], ALU.mult, ALU.add)\
                        .then_inc(idx_ready, 1)

            def weights_of_choice(b):
                dve.wait_ge(g_exp, b + 1)
                g3 = G[:, b, :].rearrange("p (h k) -> p h k", k=TOPK)
                link(nc.vector.reduce_sum(SMALL[:, 8:16], g3, AXX))
                link(nc.vector.reciprocal(SMALL[:, 8:16], SMALL[:, 8:16]))
                last = tt(g3, g3, bc(SMALL[:, 8:16], 2, TOPK), ALU.mult)
                if b >= HB:
                    last.then_inc(sel_ready, 1)
                    dve.wait_ge(sel_ready, b - HB + 1)
                else:
                    link(last)

            for step, i in ATT:
                b = i // DH
                if step == "A":
                    maps = BANKS[:, 4 + 2 * (i % 2):6 + 2 * (i % 2), :]
                    dve.wait_ge(sc_full, 2 * i + 2)
                    link(nc.vector.memset(maps[0:64, :, b * P + 64:(b + 1) * P], NEG))
                    link(nc.vector.reduce_max(MX[:, i % 2, :], maps[:, :, 0:P * (b + 1)], AXX))
                    if i >= 2:
                        dve.wait_ge(exp_done, 2 * (i - 1))
                    ts(NMX[:, i % 2, :], MX[:, i % 2, :], -(QKD ** -0.5), None, ALU.mult).then_inc(mx_ready, 1)
                    dve.wait_ge(mx_ready, i + 1)
                elif step == "B":
                    n = P * (b + 1)
                    dve.wait_ge(exp_done, 2 * i + 2)
                    link(nc.vector.reciprocal(RS[:, 0:1], SUMS[:, i, 1:2]))
                    link(stt(RS[:, 0:1], SUMS[:, i, 0:1], LAM[:, 4:5], RS[:, 0:1], ALU.mult, ALU.mult))
                    stt(PP[:, i % 2, 0, 0:n], PP[:, i % 2, 1, 0:n], RS[:, 0:1], PP[:, i % 2, 0, 0:n],
                        ALU.mult, ALU.add).then_inc(at_ready, 1)
                    dve.wait_ge(at_ready, i + 1)
                elif step == "N":
                    b = i
                    dve.wait_ge(pv_full, DH * (b + 1))
                    yd = Y[:, b, SSDW:DM]
                    link(nc.vector.reciprocal(RS[:, :], SUMS[:, b * DH:(b + 1) * DH, 0]))
                    tt(yd.rearrange("p (h d) -> p h d", d=VD), PS[2][:, :].rearrange("p (h d) -> p h d", d=VD),
                       bc(RS[:, :], 2, VD), ALU.mult).then_inc(o_free, 1)
                    dve.wait_ge(o_free, b + 1)
                    link(tt(TMP[:, 1, :], yd, yd, ALU.mult))
                    link(nc.vector.reduce_sum(SMALL[:, 2:6], TMP[:, 1, :].rearrange("p (g d) -> p g d", d=VD), AXX))
                    ts(SMALL[:, 0:2], SMALL[:, 16 + NG * b:16 + NG * (b + 1)], 1.0 / 256, EPS, ALU.mult, ALU.add)
                    link(ts(SMALL[:, 2:6], SMALL[:, 2:6], 1.0 / VD, EPS, ALU.mult, ALU.add))
                    nc.vector.reciprocal(SMALL[:, 0:6], SMALL[:, 0:6]).then_inc(yrs_half, 1)
                    dve.wait_ge(yrs_done, 2 + b + 1)
                    y3 = Y[:, b, 0:SSDW].rearrange("p (g d) -> p g d", g=NG)
                    tt(y3, y3, bc(SMALL[:, 0:2], 2, 256), ALU.mult)
                    y3 = yd.rearrange("p (g d) -> p g d", d=VD)
                    tt(y3, y3, bc(SMALL[:, 2:6], 2, VD), ALU.mult).then_inc(y_ready, 1)
                    dve.wait_ge(y_ready, y_count(1, b))
                elif step == "T":
                    evacuate_transposes(1, i)
                elif step == "U":
                    evacuate_transposes(2, i)
                elif step in ("R0", "R1"):
                    c0 = int(step[1])
                    dve.wait_ge(res_full, 2 * i + c0 + 1)
                    xb = X[:, i, c0 * HALF:(c0 + 1) * HALF]
                    tt(xb, xb, PS[c0][:, :], ALU.add).then_inc(res_free, 1)
                elif step == "r":
                    choose(i // PH, i % PH)
                elif step == "L":
                    keys_of_choice(i)
                elif step == "F":
                    dve.wait_ge(sq_done, NB + i + 1)
                    inverse_mean(SS[:, i:i + 1], SS[:, i:i + 1], DM).then_inc(rs_half, 1)
                    dve.wait_ge(rs_done, 2 + i)
                    dve.wait_ge(ld_fw, 16)
                    stt(Y[:, i, :], X[:, i, :], SS[:, i:i + 1], FW[:, :], ALU.mult, ALU.mult).then_inc(y_ready, 1)

            def use_rows(seg, it, step, first, n):
                b = seg // 2
                for r in range(first, first + n):
                    place, k = r % RING, it * step + r
                    dve.wait_ge(row_in[place], it * (step * 16 // RING) + 16 * ((NSLOT * seg + r) // RING + 1))
                    if seg % 2 == 0:
                        acc = H[:, bass.ds(k, 1)]
                        stt(UV[:, place, :], UV[:, place, :], 1.0, Y[:, b, :], ALU.mult, ALU.mult,
                            accum_out=acc).then_inc(used, 1)
                    else:
                        dve.wait_ge(used, k + NSLOT * seg)
                        weight = GH[:, bass.ds(k, 1)]
                        stt(X[:, b, :], UV[:, place, :], weight, X[:, b, :], ALU.mult, ALU.add).then_inc(used, 1)

            per_head = NSLOT // (HB * PH)
            for n in range(HB * PH):
                choose(HB + n // PH, n % PH)
                with dve.Fori(n * per_head // RING, (n + 1) * per_head // RING, 1) as it:
                    use_rows(0, it, RING, 0, RING)
                if n % PH == PH - 1:
                    keys_of_choice(HB + n // PH)
                    weights_of_choice(HB + n // PH)
            weights_of_choice(0)
            weights_of_choice(1)
            dve.wait_ge(used, NSLOT)
            nc.vector.tensor_copy(GH[:, :], H[:, :]).then_inc(h_ready, 1)

            iota = CONST[:, C_IOTA:C_IOTA + NKEY]

            def onehots(it, first):
                for q in range(2):
                    if not first:
                        dve.wait_ge(gb_full, it * 2 + (q - 1))
                    t0 = (it * 2 + q) * NG_TOK
                    tt(ONEHOT[:, q, :, 0, :], bc(iota, 1, NG_TOK), bc(KT3[:, 0, bass.ds(t0, NG_TOK)], 2, NKEY),
                       ALU.is_equal)
                    for i in range(NG_TOK):
                        t = t0 + i
                        last = ts(ONEHOT[:, q, i, 1, :], iota, KT3[:, 1, bass.ds(t, 1)],
                                  KT3[:, 2, bass.ds(t, 1)], ALU.is_equal, ALU.mult)
                    last.then_inc(oh_ready, 1)

            dve.wait_ge(selt_done, HB)
            onehots(0, True)
            with dve.Fori(1, HT // NG_TOK // 2, 1) as it:
                onehots(it, False)
            dve.wait_ge(gb_done, HT // NG_TOK)

            def weigh(it, step, j):
                dve.wait_ge(ge_done, it * step + (j + 1))
                tt(GE[:, j % 2, :], GE[:, j % 2, :], GD[:, :, bass.ds(it * step + j, 1)].rearrange("p t j -> p (t j)"),
                   ALU.mult).then_inc(yd_ready, 1)

            dve.wait_ge(gelu_done, 1)
            link(tt(GH[:, :], G[:, 0, :], H[:, :], ALU.mult))
            for seg in range(1, 2 * HB):
                j0 = 2 * SEGPAIRS * (seg - 1)
                with dve.Fori(0, QUADS, 1) as it:
                    for q in range(4):
                        weigh(it, 4, j0 + q)
                        use_rows(seg, it, QROWS, q * QROWS // 4, QROWS // 4)
                for q in range(2):
                    weigh(0, 0, j0 + 4 * QUADS + q)
                    use_rows(seg, 0, 0, QROWS * QUADS + q * LAST // 2, LAST // 2)
                dve.wait_ge(used, NSLOT * (seg + 1))
                if seg % 2 == 0:
                    nc.vector.tensor_copy(GH[:, :], H[:, :]).then_inc(h_ready, 1)
                    dve.wait_ge(gelu_done, seg // 2 + 1)
                    link(tt(GH[:, :], G[:, seg // 2, :], H[:, :], ALU.mult))
                else:
                    nc.vector.tensor_copy(SMALL[:, 0:2], SMALL[:, 2:4]).then_inc(out_ready, 1)
            for j in range(NKEY - 2 * TAIL, NKEY):
                weigh(0, 0, j)
            dve.wait_ge(vd_full, NKEY)
            for t in range(HB):
                for n in range(2):
                    xb = X[:, HB + t, n * HALF:(n + 1) * HALF]
                    last = tt(xb, xb, PS[4 + 2 * t + n][:, :], ALU.add)
                last.then_inc(out_ready, 1)

        @block.gpsimd
        def _(pool):
            def fetch(b, table, group, it, first):
                for half in range(2):
                    nc.gpsimd.tensor_copy(IXC[:, half, :], IDX[:, b, bass.ds(it * (2 * STEP) + half * STEP, STEP)])\
                        .then_inc(ixc_ready, 1)
                    pool.wait_ge(ixc_ready, it * 2 + (group + half + 1))
                    for r in range(STEP):
                        if not first or half or r >= RING:
                            pool.wait_ge(used, use)
                            pool.reg_add(use, use, 1)
                        pool.indirect_dma_start(UV[:, r % RING, :], None, table,
                                                bass.IndirectOffsetOnAxis(IXC[:, half, r:r + 1], 0))\
                            .then_inc(row_in[r % RING], 16)

            use = pool.alloc_register("use")
            pool.reg_mov(use, 1)
            group = 0
            for b in range(HB):
                pool.wait_ge(idx_ready, b + 1)
                for table in (u, v):
                    start = 1 if group == 0 else 0
                    if start:
                        fetch(b, table, group, 0, True)
                    with pool.Fori(start, NSLOT // (2 * STEP), 1) as it:
                        fetch(b, table, group, it, False)
                    group += NSLOT // STEP


def kernel(**inputs):
    import concourse.bacc as bacc
    from concourse.bass_utils import run_bass_kernel_spmd as run

    f = {k: np.asarray(a) for k, a in inputs.items()}
    vec = lambda name: f[name].reshape(-1)
    rows = np.concatenate([vec(n) for n in ("dt_bias", "a_log", "d_skip", "q_norm_w", "k_norm_w",
                                            "lambda_q1", "lambda_k1", "lambda_q2", "lambda_k2")])
    cols = np.concatenate([
        vec("mix_norm_w").reshape(8, P).T, vec("ssd_norm_w").reshape(4, P).T, vec("subln_w").reshape(1, P).T,
        f["conv_w"][0].T.reshape(CB, P, CONVW).transpose(1, 0, 2).reshape(P, CB * CONVW),
        vec("conv_b").reshape(CB, P).T], axis=1)
    inv = np.power(np.float32(500000.0), -np.arange(0, 16, 2, dtype=np.float32) / np.float32(16))
    ang = np.arange(SEQ, dtype=np.float32)[:, None] * inv[None, :].astype(np.float32)
    table = lambda t: t.astype(np.float32).reshape(NB, P, RD).transpose(1, 0, 2).reshape(P, NB * RD)
    consts = np.concatenate([np.eye(P, dtype=np.float32), np.triu(np.ones((P, P), np.float32)),
                             table(np.cos(ang)), table(np.sin(ang)),
                             np.broadcast_to(np.arange(NKEY, dtype=np.float32), (P, NKEY))], axis=1)
    arrays = {
        "x": f["x"][0], "w_in": f["w_in"][0], "w_out": f["w_out"][0], "w_q": f["peer_w_q"][0],
        "keys_t": f["peer_sub_keys"][0].reshape(2 * PH, NKEY, P).transpose(2, 0, 1),
        "u": f["peer_u"][0],
        "u_t": f["peer_u"][0].reshape(NKEY, NKEY, KC, P).transpose(1, 3, 2, 0).reshape(NKEY, P, DM),
        "v": f["peer_v"][0], "rows": np.broadcast_to(rows, (P, NROW)),
        "ffn_w": np.broadcast_to(vec("ffn_norm_w"), (P, DM)), "cols": cols, "consts": consts,
    }
    arrays = {k: np.ascontiguousarray(a) for k, a in arrays.items()}
    nc = bacc.Bacc("TRN2", target_bir_lowering=False, num_devices=1)
    args = [nc.dram_tensor(k, a.shape, F32, kind="ExternalInput").ap() for k, a in arrays.items()]
    args.append(nc.dram_tensor("out", (SEQ, DM), F32, kind="ExternalOutput").ap())
    block_program(nc, *args)
    r = run(nc, [arrays], core_ids=[0])
    return r.results[0]["out"].reshape(1, SEQ, DM)
```
